# Optimizing a Trainium2 kernel written in Bass

```python
import jax, jax.numpy as jnp
from jax import lax
import numpy as np

D_MODEL = 1024
BATCH = 1
SEQ = 512
DEPTH = 1

HEAD_DIM = 64
NA_HEADS = 8
NB_HEADS = 8
NB_KV_HEADS = 2
GRID_W = 64
NA_KH_MAX = 8
NA_KW = 16
WIN = 128
BLOCK = 128
ROPE_THETA = 10000.0
D_FF = 2816
EPS = 1e-6

WIDTH_A = NA_HEADS * HEAD_DIM
WIDTH_BQ = NB_HEADS * HEAD_DIM
WIDTH_BKV = NB_KV_HEADS * HEAD_DIM
D_IN = 3 * WIDTH_A + WIDTH_BQ + 2 * WIDTH_BKV + 2 * D_MODEL
SPLITS = (WIDTH_A, 2 * WIDTH_A, 3 * WIDTH_A,
          3 * WIDTH_A + WIDTH_BQ,
          3 * WIDTH_A + WIDTH_BQ + WIDTH_BKV,
          3 * WIDTH_A + WIDTH_BQ + 2 * WIDTH_BKV,
          3 * WIDTH_A + WIDTH_BQ + 2 * WIDTH_BKV + D_MODEL)


def rms_norm(x, g):
    xf = x.astype(jnp.float32)
    y = xf * lax.rsqrt(jnp.mean(xf * xf, axis=-1, keepdims=True) + EPS)
    return (y * g.astype(jnp.float32)).astype(x.dtype)

def swiglu(x, w_gate, w_up, w_down):
    return (jax.nn.silu(x @ w_gate) * (x @ w_up)) @ w_down

def rope(x, pos):
    half = x.shape[-1] // 2
    inv = ROPE_THETA ** (-jnp.arange(half, dtype=jnp.float32) / half)
    ang = pos.astype(jnp.float32)[:, None] * inv[None, :]
    cos = jnp.cos(ang)[None, :, None, :]
    sin = jnp.sin(ang)[None, :, None, :]
    x1 = x[..., :half].astype(jnp.float32)
    x2 = x[..., half:].astype(jnp.float32)
    out = jnp.concatenate([x1 * cos - x2 * sin, x2 * cos + x1 * sin], axis=-1)
    return out.astype(x.dtype)

def neighbourhood_attention_2d(q, k, v, rpb):
    B, T, H, dh = q.shape
    rows = T // GRID_W
    kh = min(NA_KH_MAX, rows)
    q = q.reshape(B, rows, GRID_W, H, dh)
    k = k.reshape(B, rows, GRID_W, H, dh)
    v = v.reshape(B, rows, GRID_W, H, dh)
    cols = jnp.arange(GRID_W)
    col_start = jnp.clip(cols - NA_KW // 2, 0, GRID_W - NA_KW)
    col_idx = col_start[:, None] + jnp.arange(NA_KW)[None, :]
    col_off = col_idx - cols[:, None] + (NA_KW - 1)
    rpb = rpb.astype(jnp.float32)
    scale = dh ** -0.5

    def row_block(args):
        r, q_r = args
        rs = jnp.clip(r - kh // 2, 0, rows - kh)
        k_slab = lax.dynamic_slice_in_dim(k, rs, kh, axis=1)
        v_slab = lax.dynamic_slice_in_dim(v, rs, kh, axis=1)
        k_g = k_slab[:, :, col_idx]
        v_g = v_slab[:, :, col_idx]
        row_off = rs + jnp.arange(kh) - r + (NA_KH_MAX - 1)
        bias = rpb[:, row_off[None, :, None], col_off[:, None, :]]
        s = jnp.einsum('bchd,bicjhd->bhcij', q_r, k_g).astype(jnp.float32) * scale
        s = s + bias[None]
        p = jax.nn.softmax(s.reshape(B, H, GRID_W, kh * NA_KW), axis=-1)
        p = p.reshape(B, H, GRID_W, kh, NA_KW).astype(v.dtype)
        return jnp.einsum('bhcij,bicjhd->bchd', p, v_g)

    out = lax.map(row_block, (jnp.arange(rows), jnp.moveaxis(q, 1, 0)))
    return jnp.moveaxis(out, 0, 1).reshape(B, T, H * dh)

def windowed_gqa_sink(q, k, v, sink):
    B, T, Hq, dh = q.shape
    Hkv = k.shape[2]
    G = Hq // Hkv
    nb = T // BLOCK
    qb = q.reshape(B, nb, BLOCK, Hkv, G, dh)

    def band(a):
        ap = jnp.pad(a, ((0, 0), (BLOCK, BLOCK), (0, 0), (0, 0)))
        ab = ap.reshape(B, nb + 2, BLOCK, Hkv, dh)
        return jnp.concatenate([ab[:, :-2], ab[:, 1:-1], ab[:, 2:]], axis=2)

    kb = band(k)
    vb = band(v)
    qpos = jnp.arange(nb)[:, None] * BLOCK + jnp.arange(BLOCK)[None, :]
    kpos = jnp.arange(nb)[:, None] * BLOCK - BLOCK + jnp.arange(3 * BLOCK)[None, :]
    kp = kpos[:, None, :]
    mask = (jnp.abs(qpos[:, :, None] - kp) <= WIN) & (kp >= 0) & (kp < T)
    s = jnp.einsum('bnqhgd,bnkhd->bnhgqk', qb, kb).astype(jnp.float32) * (dh ** -0.5)
    s = jnp.where(mask[None, :, None, None], s, -jnp.inf)
    sink_l = sink.astype(jnp.float32).reshape(Hkv, G)[None, None, :, :, None, None]
    m = jnp.maximum(jnp.max(s, axis=-1, keepdims=True), sink_l)
    e = jnp.exp(s - m)
    p = e / (jnp.sum(e, axis=-1, keepdims=True) + jnp.exp(sink_l - m))
    o = jnp.einsum('bnhgqk,bnkhd->bnqhgd', p.astype(v.dtype), vb)
    return o.reshape(B, T, Hq * dh)

def first_inputs(seed: int = 0) -> dict:
    key = jax.random.key(seed)
    ks = jax.random.split(key, 20)
    f32 = jnp.float32

    def w(k, shape, fan_in):
        return jax.random.normal(k, shape, f32) * (fan_in ** -0.5)

    def gain(k, shape):
        return 1.0 + 0.02 * jax.random.normal(k, shape, f32)

    return {
        "x": jax.random.normal(ks[0], (BATCH, SEQ, D_MODEL), f32),
        "ffn1_norm": gain(ks[1], (DEPTH, D_MODEL)),
        "ffn1_w_gate": w(ks[2], (DEPTH, D_MODEL, D_FF), D_MODEL),
        "ffn1_w_up": w(ks[3], (DEPTH, D_MODEL, D_FF), D_MODEL),
        "ffn1_w_down": w(ks[4], (DEPTH, D_FF, D_MODEL), D_FF),
        "mix_norm": gain(ks[5], (DEPTH, D_MODEL)),
        "w_in": w(ks[6], (DEPTH, D_MODEL, D_IN), D_MODEL),
        "na_rpb": 0.1 * jax.random.normal(ks[7], (DEPTH, NA_HEADS, 2 * NA_KH_MAX - 1, 2 * NA_KW - 1), f32),
        "sink_logit": 0.5 * jax.random.normal(ks[8], (DEPTH, NB_HEADS), f32),
        "w_branch_a": w(ks[9], (DEPTH, WIDTH_A, D_MODEL), WIDTH_A),
        "w_branch_b": w(ks[10], (DEPTH, WIDTH_BQ, D_MODEL), WIDTH_BQ),
        "w_out": w(ks[11], (DEPTH, D_MODEL, D_MODEL), D_MODEL),
        "ffn2_norm": gain(ks[12], (DEPTH, D_MODEL)),
        "ffn2_w_gate": w(ks[13], (DEPTH, D_MODEL, D_FF), D_MODEL),
        "ffn2_w_up": w(ks[14], (DEPTH, D_MODEL, D_FF), D_MODEL),
        "ffn2_w_down": w(ks[15], (DEPTH, D_FF, D_MODEL), D_FF),
        "final_norm": gain(ks[16], (D_MODEL,)),
    }

def first_block(x, ffn1_norm, ffn1_w_gate, ffn1_w_up, ffn1_w_down, mix_norm, w_in, na_rpb,
              sink_logit, w_branch_a, w_branch_b, w_out, ffn2_norm, ffn2_w_gate, ffn2_w_up,
              ffn2_w_down, final_norm):
    B, T, _ = x.shape
    pos = jnp.arange(T)
    h = x
    for l in range(DEPTH):
        h = h + 0.5 * swiglu(rms_norm(h, ffn1_norm[l]), ffn1_w_gate[l], ffn1_w_up[l], ffn1_w_down[l])
        u = rms_norm(h, mix_norm[l])
        z = u @ w_in[l]
        qa, ka, va, qb, kb, vb, ga, gb = jnp.split(z, SPLITS, axis=-1)
        qa = qa.reshape(B, T, NA_HEADS, HEAD_DIM)
        ka = ka.reshape(B, T, NA_HEADS, HEAD_DIM)
        va = va.reshape(B, T, NA_HEADS, HEAD_DIM)
        ya = neighbourhood_attention_2d(qa, ka, va, na_rpb[l])
        qb = rope(qb.reshape(B, T, NB_HEADS, HEAD_DIM), pos)
        kb = rope(kb.reshape(B, T, NB_KV_HEADS, HEAD_DIM), pos)
        vb = vb.reshape(B, T, NB_KV_HEADS, HEAD_DIM)
        yb = windowed_gqa_sink(qb, kb, vb, sink_logit[l])
        merged = jax.nn.sigmoid(ga) * (ya @ w_branch_a[l]) + jax.nn.sigmoid(gb) * (yb @ w_branch_b[l])
        h = h + merged @ w_out[l]
        h = h + 0.5 * swiglu(rms_norm(h, ffn2_norm[l]), ffn2_w_gate[l], ffn2_w_up[l], ffn2_w_down[l])
    return rms_norm(h, final_norm)


DEPTH_2 = 2

N_MIXERS = 2
CONV_K = 4
M_INNER = 2 * D_MODEL
M_HEADS = 4
M_DV = M_INNER // M_HEADS
M_DK = M_DV // 2
M_CHUNK = 64
R_WIDTH = 3 * D_MODEL // 2
R_BLOCKS = 8
R_BS = R_WIDTH // R_BLOCKS
LRU_C = 8.0

N_A = (DEPTH_2 + 1) // 2
N_B = DEPTH_2 // 2


def rmsnorm(x, g):
    xf = x.astype(jnp.float32)
    y = xf * lax.rsqrt(jnp.mean(xf * xf, axis=-1, keepdims=True) + EPS)
    return (y * g.astype(jnp.float32)).astype(x.dtype)

def causal_dwconv(x, w, b):
    s = x.shape[1]
    xp = jnp.pad(x, ((0, 0), (CONV_K - 1, 0), (0, 0)))
    y = b + xp[:, 0:s] * w[0]
    for j in range(1, CONV_K):
        y = y + xp[:, j:j + s] * w[j]
    return y

def mlstm_chunkwise(q, k, v, log_i, log_f):
    b, h, s, dk = q.shape
    dv = v.shape[-1]
    L = M_CHUNK
    nc = s // L

    def to_chunks(t):
        t = t.reshape((b, h, nc, L) + t.shape[3:])
        return jnp.moveaxis(t, 2, 0)

    qc, kc, vc, ic, fc = (to_chunks(t) for t in (q, k, v, log_i, log_f))
    causal = jnp.tril(jnp.ones((L, L), dtype=bool))

    def step(carry, inp):
        C, n, m = carry
        qb, kb, vb, ib, fb = inp
        F = jnp.cumsum(fb, axis=-1)
        D = F[..., :, None] - F[..., None, :] + ib[..., None, :]
        D = jnp.where(causal, D, -jnp.inf)
        m_t = jnp.maximum(F + m[..., None], jnp.max(D, axis=-1))
        decay = jnp.exp(F + m[..., None] - m_t)
        W = jnp.exp(D - m_t[..., None])
        Sm = jnp.einsum('bhtk,bhsk->bhts', qb, kb) * W
        num = (decay[..., None] * jnp.einsum('bhtk,bhkv->bhtv', qb, C)
               + jnp.einsum('bhts,bhsv->bhtv', Sm, vb))
        den = decay * jnp.einsum('bhtk,bhk->bht', qb, n) + jnp.sum(Sm, axis=-1)
        hb = num / jnp.maximum(jnp.abs(den), jnp.exp(-m_t))[..., None]
        w_last = W[..., -1, :]
        d_last = decay[..., -1]
        C_new = d_last[..., None, None] * C + jnp.einsum('bhs,bhsk,bhsv->bhkv', w_last, kb, vb)
        n_new = d_last[..., None] * n + jnp.einsum('bhs,bhsk->bhk', w_last, kb)
        return (C_new, n_new, m_t[..., -1]), hb

    init = (jnp.zeros((b, h, dk, dv), jnp.float32),
            jnp.zeros((b, h, dk), jnp.float32),
            jnp.zeros((b, h), jnp.float32))
    _, hs = lax.scan(step, init, (qc, kc, vc, ic, fc))
    return jnp.moveaxis(hs, 0, 2).reshape(b, h, s, dv)

def mlstm_mixer(u, w_in, conv_w, conv_b, w_q, w_k, w_v, b_i, b_f, norm_w, skip, w_out):
    bsz, s, _ = u.shape
    proj = u @ w_in
    xm, z, o_pre, i_pre, f_pre = jnp.split(
        proj, [M_INNER, 2 * M_INNER, 3 * M_INNER, 3 * M_INNER + M_HEADS], axis=-1)
    xc = jax.nn.silu(causal_dwconv(xm, conv_w, conv_b))
    xch = xc.reshape(bsz, s, M_HEADS, M_DV)
    xmh = xm.reshape(bsz, s, M_HEADS, M_DV)
    q = jnp.einsum('bshd,hde->bhse', xch, w_q).astype(jnp.float32) * (M_DK ** -0.5)
    k = jnp.einsum('bshd,hde->bhse', xch, w_k).astype(jnp.float32)
    v = jnp.einsum('bshd,hde->bhse', xmh, w_v).astype(jnp.float32)
    log_i = jnp.transpose((i_pre + b_i).astype(jnp.float32), (0, 2, 1))
    log_f = jnp.transpose(jax.nn.log_sigmoid((f_pre + b_f).astype(jnp.float32)), (0, 2, 1))
    h_tilde = jnp.transpose(mlstm_chunkwise(q, k, v, log_i, log_f), (0, 2, 1, 3))
    o = jax.nn.sigmoid(o_pre.astype(jnp.float32)).reshape(bsz, s, M_HEADS, M_DV)
    hh = o * h_tilde
    mu = jnp.mean(hh, axis=-1, keepdims=True)
    var = jnp.mean(jnp.square(hh - mu), axis=-1, keepdims=True)
    hn = ((hh - mu) * lax.rsqrt(var + EPS)).reshape(bsz, s, M_INNER)
    hn = (hn * norm_w.astype(jnp.float32)).astype(u.dtype)
    y = (hn + skip * xc) * jax.nn.silu(z)
    return y @ w_out

def linear_scan(a, bt):
    def step(hc, ab):
        a_t, b_t = ab
        hc = a_t * hc + b_t
        return hc, hc
    h0 = jnp.zeros((a.shape[0], a.shape[2]), jnp.float32)
    _, hs = lax.scan(step, h0, (jnp.moveaxis(a, 1, 0), jnp.moveaxis(bt, 1, 0)))
    return jnp.moveaxis(hs, 0, 1)

def rglru_mixer(u, w_in, conv_w, conv_b, w_a, b_a, w_x, b_x, lam, w_out):
    bsz, s, _ = u.shape
    proj = u @ w_in
    xr, g = jnp.split(proj, [R_WIDTH], axis=-1)
    xc = causal_dwconv(xr, conv_w, conv_b)
    xb = xc.reshape(bsz, s, R_BLOCKS, R_BS)
    r = jax.nn.sigmoid(jnp.einsum('bsnc,ncd->bsnd', xb, w_a).reshape(bsz, s, R_WIDTH) + b_a)
    ig = jax.nn.sigmoid(jnp.einsum('bsnc,ncd->bsnd', xb, w_x).reshape(bsz, s, R_WIDTH) + b_x)
    log_a = -LRU_C * r.astype(jnp.float32) * jax.nn.softplus(-lam.astype(jnp.float32))
    a = jnp.exp(log_a)
    bt = jnp.sqrt(-jnp.expm1(2.0 * log_a)) * (ig * xc).astype(jnp.float32)
    hs = linear_scan(a, bt).astype(u.dtype)
    y = hs * jax.nn.silu(g)
    return y @ w_out

def second_inputs(seed: int = 0) -> dict:
    key = jax.random.key(seed)
    ks = iter(jax.random.split(key, 32))
    nrm = lambda shape, scale: jax.random.normal(next(ks), shape, jnp.float32) * scale
    i_w = 3 * M_INNER + 2 * M_HEADS
    lam_u = jax.random.uniform(next(ks), (N_B, R_WIDTH), jnp.float32, 0.9, 0.999)
    sig = lam_u ** (1.0 / LRU_C)
    b_f = jnp.broadcast_to(jnp.linspace(3.0, 6.0, M_HEADS, dtype=jnp.float32), (N_A, M_HEADS))
    return {
        "x": nrm((BATCH, SEQ, D_MODEL), 1.0),
        "ln_g": 1.0 + nrm((DEPTH_2, D_MODEL), 0.05),
        "final_g": 1.0 + nrm((D_MODEL,), 0.05),
        "m_w_in": nrm((N_A, D_MODEL, i_w), D_MODEL ** -0.5),
        "m_conv_w": nrm((N_A, CONV_K, M_INNER), CONV_K ** -0.5),
        "m_conv_b": nrm((N_A, M_INNER), 0.02),
        "m_w_q": nrm((N_A, M_HEADS, M_DV, M_DK), M_DV ** -0.5),
        "m_w_k": nrm((N_A, M_HEADS, M_DV, M_DK), M_DV ** -0.5),
        "m_w_v": nrm((N_A, M_HEADS, M_DV, M_DV), M_DV ** -0.5),
        "m_b_i": nrm((N_A, M_HEADS), 0.1),
        "m_b_f": b_f + nrm((N_A, M_HEADS), 0.1),
        "m_norm_w": 1.0 + nrm((N_A, M_INNER), 0.05),
        "m_skip": 1.0 + nrm((N_A, M_INNER), 0.05),
        "m_w_out": nrm((N_A, M_INNER, D_MODEL), M_INNER ** -0.5),
        "r_w_in": nrm((N_B, D_MODEL, 2 * R_WIDTH), D_MODEL ** -0.5),
        "r_conv_w": nrm((N_B, CONV_K, R_WIDTH), CONV_K ** -0.5),
        "r_conv_b": nrm((N_B, R_WIDTH), 0.02),
        "r_w_a": nrm((N_B, R_BLOCKS, R_BS, R_BS), R_BS ** -0.5),
        "r_b_a": nrm((N_B, R_WIDTH), 0.02),
        "r_w_x": nrm((N_B, R_BLOCKS, R_BS, R_BS), R_BS ** -0.5),
        "r_b_x": nrm((N_B, R_WIDTH), 0.02),
        "r_lam": jnp.log(sig / (1.0 - sig)),
        "r_w_out": nrm((N_B, R_WIDTH, D_MODEL), R_WIDTH ** -0.5),
    }

def second_block(x, ln_g, final_g, m_w_in, m_conv_w, m_conv_b, m_w_q, m_w_k, m_w_v, m_b_i, m_b_f,
              m_norm_w, m_skip, m_w_out, r_w_in, r_conv_w, r_conv_b, r_w_a, r_b_a, r_w_x, r_b_x,
              r_lam, r_w_out):
    for layer in range(DEPTH_2):
        u = rmsnorm(x, ln_g[layer])
        j = layer // N_MIXERS
        if layer % N_MIXERS == 0:
            y = mlstm_mixer(u, m_w_in[j], m_conv_w[j], m_conv_b[j], m_w_q[j], m_w_k[j], m_w_v[j],
                            m_b_i[j], m_b_f[j], m_norm_w[j], m_skip[j], m_w_out[j])
        else:
            y = rglru_mixer(u, r_w_in[j], r_conv_w[j], r_conv_b[j], r_w_a[j], r_b_a[j],
                            r_w_x[j], r_b_x[j], r_lam[j], r_w_out[j])
        x = x + y
    return rmsnorm(x, final_g)


def setup_inputs(seed=0):
    out = dict(first_inputs(seed))
    for name, value in second_inputs(seed + 1).items():
        if name != "x":
            out[name + "_2"] = value
    return out


def reference(
    x, ffn1_norm, ffn1_w_gate, ffn1_w_up, ffn1_w_down, mix_norm, w_in, na_rpb, sink_logit,
    w_branch_a, w_branch_b, w_out, ffn2_norm, ffn2_w_gate, ffn2_w_up, ffn2_w_down, final_norm,
    ln_g_2, final_g_2, m_w_in_2, m_conv_w_2, m_conv_b_2, m_w_q_2, m_w_k_2, m_w_v_2, m_b_i_2,
    m_b_f_2, m_norm_w_2, m_skip_2, m_w_out_2, r_w_in_2, r_conv_w_2, r_conv_b_2, r_w_a_2,
    r_b_a_2, r_w_x_2, r_b_x_2, r_lam_2, r_w_out_2,
):
    x = first_block(
        x, ffn1_norm, ffn1_w_gate, ffn1_w_up, ffn1_w_down, mix_norm, w_in, na_rpb, sink_logit,
        w_branch_a, w_branch_b, w_out, ffn2_norm, ffn2_w_gate, ffn2_w_up, ffn2_w_down,
        final_norm,
    )
    return second_block(
        x, ln_g_2, final_g_2, m_w_in_2, m_conv_w_2, m_conv_b_2, m_w_q_2, m_w_k_2, m_w_v_2,
        m_b_i_2, m_b_f_2, m_norm_w_2, m_skip_2, m_w_out_2, r_w_in_2, r_conv_w_2, r_conv_b_2,
        r_w_a_2, r_b_a_2, r_w_x_2, r_b_x_2, r_lam_2, r_w_out_2,
    )


_drawn_inputs = setup_inputs


def setup_inputs(seed=0):
    import zlib

    import numpy as np

    out = dict(_drawn_inputs(seed))
    spreads = {}
    factors = {'ffn1_norm': 3.975,
     'mix_norm': 8.0,
     'na_rpb': 5.038,
     'sink_logit': 8.0,
     'ffn2_norm': 4.755,
     'm_conv_b_2': 3.162,
     'm_b_i_2': 64.0,
     'm_skip_2': 3.59,
     'r_b_a_2': 55.734,
     'r_b_x_2': 29.102,
     'm_norm_w_2': 3.101}
    for name, (base, spread) in spreads.items():
        noise = np.random.default_rng([zlib.crc32(name.encode()), seed]).standard_normal(out[name].shape)
        drawn = base * np.exp(spread * noise) if base else spread * noise
        out[name] = __import__('jax').numpy.asarray(drawn.astype(out[name].dtype))
    for name, factor in factors.items():
        out[name] = (out[name] * factor).astype(out[name].dtype)
    return out
```

```python
from contextlib import ExitStack, contextmanager

import concourse.bass as bass
from concourse import mybir

F32 = mybir.dt.float32
F32R = mybir.dt.float32r
ACT = mybir.ActivationFunctionType
ALU = mybir.AluOpType
AX_X = mybir.AxisListType.X

P = 128
T = 512
D = 1024
DC = D // P
UB = 8
F_CHUNKS = 22
HD = 64
SCALE = HD ** -0.5
EPS = 1e-6
LRU_C = 8.0
M_HEADS = 4
M_DV = 512
M_DK = 256
RG_CHUNKS = 12
KEY_COL0 = (0, 8, 24, 32)
BIAS_OF = (0, 1, 1, 2)

U_FFN = 2 * F_CHUNKS + 3 * DC
U_QKV = 18
U_MERGE = 3 * DC
U_WOUT = DC
U_HEAD = 20
U_PAIR = 8
U_FFN1 = 0
U_MIX = U_FFN1 + U_FFN
U_MERGE0 = U_MIX + U_QKV
U_WOUT0 = U_MERGE0 + U_MERGE
U_FFN2 = U_WOUT0 + U_WOUT
U_GATES = U_FFN2 + U_FFN
U_HEAD0 = U_GATES + 1
U_PAIR0 = U_HEAD0 + M_HEADS * U_HEAD
U_ROUT = U_PAIR0 + 4 * U_PAIR
U_END = U_ROUT + 2 * DC
U_ALL = U_END + 3

G_FFN = 2 * F_CHUNKS + DC
G_FFN1 = 0
G_MIX = G_FFN1 + G_FFN
G_MERGE0 = G_MIX + 14
G_WOUT0 = G_MERGE0 + 4 * DC
G_FFN2 = G_WOUT0 + DC
G_GATES = G_FFN2 + G_FFN
G_HEAD0 = G_GATES + 1
G_HEAD = 24
G_PAIR0 = G_HEAD0 + M_HEADS * G_HEAD
G_PAIR = 6
G_ROUT = G_PAIR0 + 4 * G_PAIR

V_FFN1, V_MIX, V_FFN2, V_FINAL, V_LN0, V_LN1, V_FINAL2 = (8 * k for k in range(7))
V_SINK = 56
V_BIF = 64
V_HEAD = 66
V_PER_HEAD = 28
V_PAIR = V_HEAD + M_HEADS * V_PER_HEAD
V_PER_PAIR = 24
V_ALL = V_PAIR + 4 * V_PER_PAIR

GATE_BLOCKS = [(0, 0), (1, 0), (0, 1), (1, 1), (2, 1), (1, 2), (2, 2)]


class Lin:

    def __init__(self, c, m=0, i=None):
        self.c, self.m, self.i = c, m, i

    def __add__(self, k):
        return Lin(self.c + k, self.m, self.i)

    def v(self, scale=1):
        return self.c * scale if self.i is None else self.i * (self.m * scale) + self.c * scale

    def half(self):
        return Lin(self.c // 2, self.m // 2, self.i)

    @property
    def slot(self):
        assert self.m % 2 == 0
        return self.c % 2


class Steps:

    def __init__(self, engine, sem):
        self.engine, self.sem, self.at = engine, sem, Lin(0)

    def __call__(self, ins):
        ins.then_inc(self.sem, 1)
        self.at = self.at + 1

    def wait(self):
        self.engine.wait_ge(self.sem, self.at.v())

    @contextmanager
    def turns(self, i, n, per):
        start = self.at.c
        self.at = Lin(start, per, i)
        yield
        assert self.at.c - start == per, (self.at.c - start, per)
        self.at = Lin(start + n * per)


def build_program(nc, x_in, w_in, vec_in, bias_in, rope_in, maskb_in, ident_in, sel_in, causal_in, out):
    ctx = ExitStack()
    with ctx:
        def sb(name, shape, dt=F32, scope=ctx):
            return scope.enter_context(nc.sbuf_tensor(name, shape, dt))

        def sem(name):
            return ctx.enter_context(nc.semaphore(name))

        x = sb("x", [P, DC, T])
        rstd = sb("rstd", [P, T])
        rms = sb("rms", [P, T])
        sq = sb("sq", [P, 2, T])
        sumsq = sb("sumsq", [P, T])
        w_raw = sb("w_raw", [P, 2, UB * P])
        w_hi = sb("w_hi", [P, 2, UB * P], F32R)
        w_lo = sb("w_lo", [P, 2, UB * P], F32R)
        u_hi = sb("u_hi", [P, DC, T], F32R)
        u_lo = sb("u_lo", [P, DC, T], F32R)
        vecs = sb("vecs", [P, V_ALL])
        ones = sb("ones", [P, P])
        ident = sb("ident", [P, P])
        eps = sb("eps", [P, 1])

        with ExitStack() as s:
            hid_hi = sb("hid_hi", [P, F_CHUNKS, T], F32R, s)
            hid_lo = sb("hid_lo", [P, F_CHUNKS, T], F32R, s)
            gate = sb("gate", [P, T], F32, s)
            gate_act = sb("gate_act", [P, T], F32, s)
            up = sb("up", [P, T], F32, s)
            hid = sb("hid", [P, T], F32, s)

        with ExitStack() as s:
            ya_hi = sb("ya_hi", [P, 4, T], F32R, s)
            ya_lo = sb("ya_lo", [P, 4, T], F32R, s)
            yb_hi = sb("yb_hi", [P, 4, T], F32R, s)
            yb_lo = sb("yb_lo", [P, 4, T], F32R, s)
            with ExitStack() as s2:
                qk_a = sb("qk_a", [P, 8, T], F32, s2)
                v_a = sb("v_a", [P, 4, T], F32, s2)
                v_win = sb("v_win", [P, 4, 2, T], F32, s2)
                qk_b = sb("qk_b", [P, 5, T], F32, s2)
                v_b = sb("v_b", [P, 4, P], F32, s2)
                bias = sb("bias", [P, 2, 3 * 256], F32, s2)
                rope = sb("rope", [P, 2, T], F32, s2)
                mask_b = sb("mask_b", [P, 3 * P], F32, s2)
                rstd_col = sb("rstd_col", [P, 4], F32, s2)
                unrot = sb("unrot", [P, T], F32, s2)
                rot_cos = sb("rot_cos", [P, T], F32, s2)
                rot_sin = sb("rot_sin", [P, T], F32, s2)
                score = sb("score", [P, 2, 384], F32, s2)
                prob = sb("prob", [P, 2, 384], F32, s2)
                prob_t = sb("prob_t", [P, 2, 384], F32, s2)
                row = sb("row", [P, 2, 8], F32, s2)
            with ExitStack() as s2:
                merged_hi = sb("merged_hi", [P, DC, T], F32R, s2)
                merged_lo = sb("merged_lo", [P, DC, T], F32R, s2)
                gate_pre = sb("gate_pre", [P, 2, T], F32, s2)
                gate_sig = sb("gate_sig", [P, 2, T], F32, s2)
                branch = sb("branch", [P, 2, T], F32, s2)
                merged = sb("merged", [P, T], F32, s2)

        with ExitStack() as s:
            neg_max = sb("neg_max", [P, M_HEADS, T], F32, s)
            floor = sb("floor", [P, M_HEADS, T], F32, s)
            a_col = sb("a_col", [P, 4, 4], F32, s)
            a_head = sb("a_head", [P, 4], F32, s)
            hvec = sb("hvec", [P, V_PER_HEAD], F32, s)
            sel = sb("sel", [4, M_HEADS, P], F32, s)
            causal = sb("causal", [P, P], F32, s)
            with ExitStack() as s2:
                g_rows = [sb(f"g_row{k}", [4, T], F32, s2) for k in range(10)]
            xm = sb("xm", [P, 4, T + 3], F32, s)
            xm_hi = sb("xm_hi", [P, 4, T], F32R, s)
            xm_lo = sb("xm_lo", [P, 4, T], F32R, s)
            xc = sb("xc", [P, 4, T], F32, s)
            xy_hi = sb("xy_hi", [P, 4, T], F32R, s)
            xy_lo = sb("xy_lo", [P, 4, T], F32R, s)
            o_sig = sb("o_sig", [P, 4, T], F32, s)
            z_act = sb("z_act", [P, 4, T], F32, s)
            q_m = sb("q_m", [P, 2, T], F32, s)
            k_m = sb("k_m", [P, 2, T], F32, s)
            v_m = sb("v_m", [P, 4, T], F32, s)
            sw = sb("sw", [P, 4, T], F32, s)
            pre = sb("pre", [P, 2, T], F32, s)
            conv = sb("conv", [P, T], F32, s)
            den = sb("den", [P, T], F32, s)
            hsum = sumsq
            hh = sb("hh", [P, 4, T], F32, s)

        with ExitStack() as s:
            ry_hi = sb("ry_hi", [P, RG_CHUNKS, T], F32R, s)
            ry_lo = sb("ry_lo", [P, RG_CHUNKS, T], F32R, s)
            xr = sb("xr", [P, 3, T + 3], F32, s)
            rc = sb("rc", [P, 3, T], F32, s)
            rc_hi = sb("rc_hi", [P, 3, T], F32R, s)
            rc_lo = sb("rc_lo", [P, 3, T], F32R, s)
            g_pre = sb("g_pre", [P, 2, T], F32, s)
            g_act = sb("g_act", [P, 3, T], F32, s)
            rgate = sb("rgate", [P, 3, T], F32, s)
            igate = sb("igate", [P, 3, T], F32, s)
            decay = sb("decay", [P, 3, T], F32, s)
            tanh = sb("tanh", [P, 3, T], F32, s)
            pvec = sb("pvec", [P, V_PER_PAIR], F32, s)
            rate = sb("rate", [P, 5, RG_CHUNKS], F32, s)
            pair_rate = sb("pair_rate", [P, 2, 3], F32, s)

        bank = [ctx.enter_context(nc.psum_tensor(f"bank{k}", [P, T], F32)) for k in range(8)]
        stat = bank[2]

        x_loaded = [sem(f"x_loaded{k}") for k in range(4)]
        vec_loaded = sem("vec_loaded")
        tab_loaded = sem("tab_loaded")
        ident_loaded = sem("ident_loaded")
        sel_loaded = sem("sel_loaded")
        causal_loaded = sem("causal_loaded")
        consts = sem("consts")
        raw_loaded = [sem("raw_loaded0"), sem("raw_loaded1")]
        hi_ready = sem("hi_ready")
        lo_ready = sem("lo_ready")
        unit_used = sem("unit_used")
        bank_read = sem("bank_read")
        sq_ready = sem("sq_ready")
        sq_added = sem("sq_added")
        stat_ready = sem("stat_ready")
        rms_ready = sem("rms_ready")
        rstd_ready = sem("rstd_ready")
        u_hi_ready = sem("u_hi_ready")
        u_lo_ready = sem("u_lo_ready")
        x_scaled = sem("x_scaled")
        gate_acted = sem("gate_acted")
        hid_ready = sem("hid_ready")
        hid_hi_ready = sem("hid_hi_ready")
        hid_lo_ready = sem("hid_lo_ready")
        rcol_ready = sem("rcol_ready")
        rcol_copied = sem("rcol_copied")
        va_ready = sem("va_ready")
        v_moved = sem("v_moved")
        rotated = sem("rotated")
        bias_loaded = [sem("bias_loaded0"), sem("bias_loaded1")]
        scored = sem("scored")
        biased = sem("biased")
        row_max_ready = sem("row_max_ready")
        exp_ready = sem("exp_ready")
        prob_ready = sem("prob_ready")
        transposed = sem("transposed")
        prob_t_ready = sem("prob_t_ready")
        attended = sem("attended")
        att_hi_ready = sem("att_hi_ready")
        att_lo_ready = sem("att_lo_ready")
        sig_ready = sem("sig_ready")
        merged_ready = sem("merged_ready")
        merged_hi_ready = sem("merged_hi_ready")
        merged_lo_ready = sem("merged_lo_ready")
        f_abs_ready = sem("f_abs_ready")
        gates_dve = sem("gates_dve")
        gates_act = sem("gates_act")
        gates_pe = sem("gates_pe")
        xm_hi_ready = sem("xm_hi_ready")
        xm_lo_ready = sem("xm_lo_ready")
        conv_ready = sem("conv_ready")
        xc_ready = sem("xc_ready")
        xc_hi_ready = sem("xc_hi_ready")
        xc_lo_ready = sem("xc_lo_ready")
        oz_ready = sem("oz_ready")
        v_m_ready = sem("v_m_ready")
        w_arg = sem("w_arg")
        w_exp = sem("w_exp")
        w_masked = sem("w_masked")
        s_ready = sem("s_ready")
        sw_ready = sem("sw_ready")
        den_ready = sem("den_ready")
        den_abs = sem("den_abs")
        num_ready = sem("num_ready")
        h_ready = sem("h_ready")
        h_summed = sem("h_summed")
        m_stat = sem("m_stat")
        h_centred = sem("h_centred")
        h_squared = sem("h_squared")
        h_sq_ready = sem("h_sq_ready")
        m_rms = sem("m_rms")
        y_ready = sem("y_ready")
        y_hi_ready = sem("y_hi_ready")
        y_lo_ready = sem("y_lo_ready")
        rate_dve = sem("rate_dve")
        rate_act = sem("rate_act")
        rconv_ready = sem("rconv_ready")
        rc_hi_ready = sem("rc_hi_ready")
        rc_lo_ready = sem("rc_lo_ready")
        g_ready = sem("g_ready")
        rgates = sem("rgates")
        r_act = sem("r_act")
        b_squared = sem("b_squared")
        b_root = sem("b_root")
        ry_ready = sem("ry_ready")
        ry_hi_ready = sem("ry_hi_ready")
        ry_lo_ready = sem("ry_lo_ready")
        vec_step = sem("vec_step")
        pool_step = sem("pool_step")
        out_ready = sem("out_ready")
        stored = sem("stored")

        block = ctx.enter_context(nc.Block())

        def grid(ap, c0, n):
            return ap.rearrange("p (r c) -> p r c", r=8)[:, :, c0:c0 + n]

        A_TILES = [("a", m, j, e) for m in range(4) for j in range(4) for e in range(2)]
        B_TILES = [("b", m, n, e) for m in range(4) for n in range(4) for e in range(2)]
        TILES = A_TILES + B_TILES

        def key_blocks(n):
            return [b for b in (n - 1, n, n + 1) if 0 <= b < 4]

        def tile_keys(t):
            kind, m, j, e = TILES[t]
            return 256 if kind == "a" else P * len(key_blocks(j))

        @block.sync
        def _(sp):
            for k in range(2):
                sp.dma_start(w_raw[:, k, :], w_in[k]).then_inc(raw_loaded[k], 16)
            with sp.Fori(1, U_ALL // 2) as i:
                for k in range(2):
                    sp.wait_ge(lo_ready, i * 2 + (k - 1))
                    sp.dma_start(w_raw[:, k, :], w_in[bass.ds(i * 2 + k, 1)].rearrange("a p c -> (a p) c"))\
                      .then_inc(raw_loaded[k], 16)
            for m in range(DC):
                sp.wait_ge(out_ready, m + 1)
                sp.dma_start(out[m * P:(m + 1) * P, :], x[:, m, :]).then_inc(stored, 16)
            sp.wait_ge(stored, 16 * DC)

        @block.tensor
        def _(pe):
            def product(o, pairs, n, last_of_unit=False, start=True, stop=True):
                ins = None
                for k, (b, hi, lo) in enumerate(pairs):
                    wh = w_hi[:, n.slot, b * P:(b + 1) * P]
                    wl = w_lo[:, n.slot, b * P:(b + 1) * P]
                    nc.tensor.matmul(o, wh, hi, start=start and k == 0, stop=False)
                    nc.tensor.matmul(o, wh, lo, start=False, stop=False)
                    ins = nc.tensor.matmul(o, wl, hi, start=False, stop=stop and k == len(pairs) - 1)
                if last_of_unit:
                    ins.then_inc(unit_used, 1)
                return ins

            def unit_ready(n):
                pe.wait_ge(lo_ready, (n + 1).v())

            def bank_free(g):
                pe.wait_ge(bank_read, (g + 1).v())

            def linear8(n, g):
                unit_ready(n)
                bank_free(g)
                product(bank[g.slot][:, :], [(k, u_hi[:, k, :], u_lo[:, k, :]) for k in range(8)], n, True)

            def norm_stat(q):
                pe.wait_ge(sq_added, 9 * (q + 1))
                if q == 0:
                    pe.wait_ge(consts, 4)
                nc.tensor.matmul(stat[:, :], ones[:, :], sumsq[:, :], start=True, stop=True).then_inc(stat_ready, 1)

            def ffn(f, q, nu, u0, g0):
                norm_stat(q)
                pe.wait_ge(u_lo_ready, 8 * (nu + 1))
                with pe.Fori(0, F_CHUNKS) as i:
                    n, g = Lin(u0, 2, i), Lin(g0, 2, i)
                    linear8(n, g)
                    linear8(n + 1, g + 1)
                pe.wait_ge(hid_lo_ready, F_CHUNKS * (f + 1))
                with pe.Fori(0, DC // 2) as i:
                    for e in range(2):
                        n, g = Lin(u0 + 2 * F_CHUNKS + 3 * e, 6, i), Lin(g0 + 2 * F_CHUNKS + e, 2, i)
                        bank_free(g)
                        for part in range(3):
                            unit_ready(n + part)
                            ks = range(8 * part, min(8 * part + 8, F_CHUNKS))
                            product(bank[g.slot][:, :], [(k - 8 * part, hid_hi[:, k, :], hid_lo[:, k, :]) for k in ks],
                                    n + part, True, start=part == 0, stop=part == 2)

            ffn(0, 0, 0, U_FFN1, G_FFN1)

            norm_stat(1)
            pe.wait_ge(u_lo_ready, 16)
            with pe.Fori(0, 4) as i:
                for e in range(2):
                    linear8(Lin(U_MIX + e, 2, i), Lin(G_MIX + e, 2, i))
            pe.wait_ge(rstd_ready, 2)
            for t in range(4):
                ins = nc.tensor.matmul(stat[:, t:t + 1], rstd[0:1, t * P:(t + 1) * P], ones[0:1, 0:1], start=True, stop=True)
            ins.then_inc(rcol_ready, 1)
            for part in range(4):
                n = Lin(U_MIX + 8 + part)
                unit_ready(n)
                for t in range(4):
                    tok = slice(t * P, (t + 1) * P)
                    for c in range(2):
                        k = 2 * part + c
                        wh, wl = w_hi[:, n.slot, c * T:(c + 1) * T], w_lo[:, n.slot, c * T:(c + 1) * T]
                        nc.tensor.matmul(bank[3 + t][:, :], u_hi[:, k, tok], wh, start=k == 0, stop=False)
                        nc.tensor.matmul(bank[3 + t][:, :], u_lo[:, k, tok], wh, start=False, stop=False)
                        ins = nc.tensor.matmul(bank[3 + t][:, :], u_hi[:, k, tok], wl, start=False, stop=k == 7)
                ins.then_inc(unit_used, 1)
            for k in range(5):
                linear8(Lin(U_MIX + 12 + k), Lin(G_MIX + 8 + k))
            n, g = Lin(U_MIX + 17), Lin(G_MIX + 13)
            unit_ready(n)
            bank_free(g)
            for t in range(4):
                tok = slice(t * P, (t + 1) * P)
                for k in range(8):
                    wh, wl = w_hi[:, n.slot, k * P:(k + 1) * P], w_lo[:, n.slot, k * P:(k + 1) * P]
                    o = bank[g.slot][:, tok]
                    nc.tensor.matmul(o, u_hi[:, k, tok], wh, start=k == 0, stop=False)
                    nc.tensor.matmul(o, u_lo[:, k, tok], wh, start=False, stop=False)
                    ins = nc.tensor.matmul(o, u_hi[:, k, tok], wl, start=False, stop=k == 7)
            ins.then_inc(unit_used, 1)

            pe.wait_ge(bank_read, G_MIX + 14 + 2)
            pe.wait_ge(va_ready, 4)
            pe.wait_ge(rotated, 5)
            pe.wait_ge(ident_loaded, 16)
            for t in range(len(TILES) + 3):
                if t < len(TILES):
                    kind, m, j, e = TILES[t]
                    half = slice(HD * e, HD * (e + 1))
                    if t >= 2:
                        pe.wait_ge(biased, t - 1)
                    o = bank[3 + t % 2][:, 0:tile_keys(t)]
                    if kind == "a":
                        q_t, k_t = qk_a[half, m, j * P:(j + 1) * P], grid(qk_a[half, 4 + m, :], KEY_COL0[j], 32)
                    else:
                        kb = key_blocks(j)
                        q_t = qk_b[half, m, j * P:(j + 1) * P]
                        k_t = qk_b[half, 4, kb[0] * P:(kb[-1] + 1) * P]
                    nc.tensor.matmul(o, q_t, k_t, start=True, stop=True).then_inc(scored, 1)
                if 2 <= t < len(TILES) + 2:
                    s = t - 2
                    pe.wait_ge(prob_ready, s + 1)
                    if s >= 2:
                        pe.wait_ge(prob_t_ready, s - 1)
                    for b in range(tile_keys(s) // P):
                        ins = nc.tensor.transpose(bank[5 + s % 2][:, b * P:(b + 1) * P], prob[:, s % 2, b * P:(b + 1) * P],
                                                  ident[:, :])
                    ins.then_inc(transposed, 1)
                if t >= 3:
                    s = t - 3
                    kind, m, j, e = TILES[s]
                    pe.wait_ge(prob_t_ready, s + 1)
                    if s == 0:
                        pe.wait_ge(v_moved, 16 * 32)
                    if e == 0 and s >= 4:
                        pe.wait_ge(att_lo_ready, s // 2 - 1)
                    o = bank[(s // 2) % 2][HD * e:HD * (e + 1), 0:P]
                    nb = tile_keys(s) // P
                    for b in range(nb):
                        if kind == "a":
                            h = 2 * m + e
                            v_t = v_win[:, j, b, h * HD:(h + 1) * HD]
                        else:
                            v_t = v_b[:, key_blocks(j)[b], e * HD:(e + 1) * HD]
                        ins = nc.tensor.matmul(o, v_t, prob_t[:, s % 2, b * P:(b + 1) * P], start=b == 0, stop=b == nb - 1)
                    ins.then_inc(attended, 1)

            pe.wait_ge(att_lo_ready, len(TILES) // 2)
            with pe.Fori(0, DC // 2) as i:
                for e in range(2):
                    n, g = Lin(U_MERGE0 + 3 * e, 6, i), Lin(G_MERGE0 + 4 * e, 8, i)
                    linear8(n, g)
                    linear8(n + 1, g + 1)
                    unit_ready(n + 2)
                    bank_free(g + 2)
                    product(bank[(g + 2).slot][:, :], [(k, ya_hi[:, k, :], ya_lo[:, k, :]) for k in range(4)], n + 2)
                    bank_free(g + 3)
                    product(bank[(g + 3).slot][:, :], [(4 + k, yb_hi[:, k, :], yb_lo[:, k, :]) for k in range(4)], n + 2, True)
            pe.wait_ge(merged_lo_ready, DC)
            with pe.Fori(0, DC // 2) as i:
                for e in range(2):
                    n, g = Lin(U_WOUT0 + e, 2, i), Lin(G_WOUT0 + e, 2, i)
                    unit_ready(n)
                    bank_free(g)
                    product(bank[g.slot][:, :], [(k, merged_hi[:, k, :], merged_lo[:, k, :]) for k in range(8)], n, True)

            ffn(1, 2, 2, U_FFN2, G_FFN2)
            norm_stat(3)
            norm_stat(4)

            pe.wait_ge(u_lo_ready, 32)
            linear8(Lin(U_GATES), Lin(G_GATES))
            pe.wait_ge(gates_dve, 1)
            pe.wait_ge(sel_loaded, 16)
            for t in range(4):
                ins = nc.tensor.matmul(bank[3][:, 4 * t:4 * t + 4], g_rows[5][:, t * P:(t + 1) * P], ident[0:4, 0:4],
                                       start=True, stop=True)
            ins.then_inc(gates_pe, 1)
            pe.wait_ge(gates_dve, 2)
            for k, (row_t, need) in enumerate(((g_rows[7], 2), (g_rows[9], 0))):
                if k == 1:
                    pe.wait_ge(gates_act, 3)
                for h in range(M_HEADS):
                    b = 4 * k + h
                    if b >= 2:
                        pe.wait_ge(gates_dve, 2 + b)
                    nc.tensor.matmul(bank[4 + b % 2][:, :], sel[:, h, :], row_t[:, :], start=True, stop=True)\
                      .then_inc(gates_pe, 1)
            with pe.Fori(0, M_HEADS) as i:
                n0, g0 = Lin(U_HEAD0, U_HEAD, i), Lin(G_HEAD0, G_HEAD, i)
                for k in range(12):
                    linear8(n0 + k, g0 + k)
                pe.wait_ge(xc_lo_ready, Lin(4, 4, i).v())
                for k in range(2):
                    n, g = n0 + 12 + k, g0 + 12 + 2 * k
                    unit_ready(n)
                    for e in range(2):
                        bank_free(g + e)
                        product(bank[(g + e).slot][:, :], [(4 * e + c, xy_hi[:, c, :], xy_lo[:, c, :]) for c in range(4)],
                                n, e == 1)
                for part in range(2):
                    n = n0 + 14 + part
                    unit_ready(n)
                    for t in range(4):
                        tok = slice(t * P, (t + 1) * P)
                        for c in range(2):
                            k = 2 * part + c
                            wh, wl = w_hi[:, n.slot, c * T:(c + 1) * T], w_lo[:, n.slot, c * T:(c + 1) * T]
                            nc.tensor.matmul(bank[3 + t][:, :], xm_hi[:, k, tok], wh, start=k == 0, stop=False)
                            nc.tensor.matmul(bank[3 + t][:, :], xm_lo[:, k, tok], wh, start=False, stop=False)
                            ins = nc.tensor.matmul(bank[3 + t][:, :], xm_hi[:, k, tok], wl, start=False, stop=k == 3)
                    ins.then_inc(unit_used, 1)
                pe.wait_ge(bank_read, (g0 + 16 + 2).v())
                pe.wait_ge(v_m_ready, Lin(4, 4, i).v())
                for si in range(4):
                    if si >= 2:
                        pe.wait_ge(sw_ready, Lin(si - 1, 4, i).v())
                    for e in range(2):
                        ins = nc.tensor.matmul(bank[3 + si % 2][:, si * P:T], k_m[:, e, si * P:(si + 1) * P],
                                               q_m[:, e, si * P:T], start=e == 0, stop=e == 1)
                    ins.then_inc(s_ready, 1)
                pe.wait_ge(sw_ready, Lin(4, 4, i).v())
                for si in range(4):
                    ins = nc.tensor.matmul(bank[5][:, si * P:T], ones[:, :], sw[:, si, si * P:T], start=si == 0, stop=si == 3)
                ins.then_inc(den_ready, 1)
                for c in range(4):
                    for si in range(4):
                        ins = nc.tensor.matmul(bank[(6, 7, 3, 4)[c]][:, si * P:T], v_m[:, si, c * P:(c + 1) * P],
                                               sw[:, si, si * P:T], start=si == 0, stop=si == 3)
                    ins.then_inc(num_ready, 1)
                for k in range(2):
                    pe.wait_ge(*((h_summed, Lin(1, 1, i).v()), (h_squared, Lin(3, 3, i).v()))[k])
                    nc.tensor.matmul(stat[:, :], ones[:, :], hsum[:, :], start=True, stop=True).then_inc(m_stat, 1)
                pe.wait_ge(y_lo_ready, Lin(4, 4, i).v())
                for k in range(4):
                    n, g = n0 + 16 + k, g0 + 16 + 2 * k
                    unit_ready(n)
                    for e in range(2):
                        bank_free(g + e)
                        product(bank[(g + e).slot][:, :], [(4 * e + c, xy_hi[:, c, :], xy_lo[:, c, :]) for c in range(4)],
                                n, e == 1)

            norm_stat(5)
            pe.wait_ge(u_lo_ready, 40)
            with pe.Fori(0, 4) as i:
                n0, g0 = Lin(U_PAIR0, U_PAIR, i), Lin(G_PAIR0, G_PAIR, i)
                for k in range(6):
                    linear8(n0 + k, g0 + k)
                pe.wait_ge(rc_lo_ready, Lin(3, 3, i).v())
                for k in range(2):
                    n = n0 + 6 + k
                    unit_ready(n)
                    for c in range(3):
                        b = (3, 4, 5, 6, 7, 2)[3 * k + c]
                        pairs = [(s, rc_hi[:, ci, :], rc_lo[:, ci, :]) for s, (ci, co) in enumerate(GATE_BLOCKS) if co == c]
                        product(bank[b][:, :], pairs, n, c == 2)
            pe.wait_ge(ry_lo_ready, RG_CHUNKS)
            with pe.Fori(0, DC // 2) as i:
                for e in range(2):
                    n, g = Lin(U_ROUT + 2 * e, 4, i), Lin(G_ROUT + e, 2, i)
                    bank_free(g)
                    for part in range(2):
                        unit_ready(n + part)
                        product(bank[g.slot][:, :],
                                [(k, ry_hi[:, 6 * part + k, :], ry_lo[:, 6 * part + k, :]) for k in range(6)],
                                n + part, True, start=part == 0, stop=part == 1)
            norm_stat(6)

        @block.scalar
        def _(act):
            for k in range(4):
                act.dma_start(x[:, 2 * k:2 * k + 2, :],
                              x_in[2 * k * P:(2 * k + 2) * P, :].rearrange("(c p) t -> p c t", p=P)).then_inc(x_loaded[k], 16)
                if k == 0:
                    act.dma_start(vecs[:, :], vec_in).then_inc(vec_loaded, 16)
            act.dma_start(ident[:, :], ident_in).then_inc(ident_loaded, 16)

            def split_raw(n):
                act.wait_ge(raw_loaded[n.slot], (n.half() + 1).v(16))
                if n.i is not None or n.c >= 2:
                    act.wait_ge(unit_used, (n + (-1)).v())
                nc.scalar.activation(w_hi[:, n.slot, :], w_raw[:, n.slot, :], ACT.Copy).then_inc(hi_ready, 1)

            def norm_chunk(q, m, nu, gcol):
                act.wait_ge(sq_added, m.v() + 9 * q if m.i is not None else 9 * q + m.c)
                nc.scalar.activation(sq[:, m.slot:m.slot + 1, :], at_chunk(x, m), ACT.Square).then_inc(sq_ready, 1)
                if nu is not None:
                    col = vecs[:, bass.ds(m.v() + gcol, 1)] if m.i is not None else vecs[:, gcol + m.c:gcol + m.c + 1]
                    nc.scalar.activation(at_chunk(u_hi, m), at_chunk(x, m), ACT.Copy, scale=col).then_inc(u_hi_ready, 1)

            def at_chunk(t, m):
                return t[:, bass.ds(m.v(), 1), :] if m.i is not None else t[:, m.c:m.c + 1, :]

            def norm_rms(q):
                act.wait_ge(stat_ready, q + 1)
                nc.scalar.activation(rms[:, :], stat[:, :], ACT.Sqrt, bias=eps[:, 0:1], scale=1.0 / D).then_inc(rms_ready, 1)

            def ffn(f, q, q_next, nu_next, gcol, u0, g0):
                norm_rms(q)
                with act.Fori(0, F_CHUNKS) as i:
                    n, g = Lin(u0, 2, i), Lin(g0, 2, i)
                    split_raw(n + 2)
                    act.wait_ge(bank_read, (g + 3).v())
                    nc.scalar.activation(gate_act[:, :], gate[:, :], ACT.Silu).then_inc(gate_acted, 1)
                    split_raw(n + 3)
                    act.wait_ge(hid_ready, Lin(f * F_CHUNKS + 1, 1, i).v())
                    nc.scalar.activation(hid_hi[:, bass.ds(i, 1), :], hid[:, :].unsqueeze(1), ACT.Copy).then_inc(hid_hi_ready, 1)
                with act.Fori(0, DC // 2) as i:
                    for e in range(2):
                        n, g = Lin(u0 + 2 * F_CHUNKS + 3 * e, 6, i), Lin(g0 + 2 * F_CHUNKS + e, 2, i)
                        for part in range(3):
                            split_raw(n + part + 2)
                        act.wait_ge(bank_read, (g + 3).v())
                        norm_chunk(q_next, Lin(e, 2, i), nu_next, gcol)

            split_raw(Lin(0))
            split_raw(Lin(1))
            act.wait_ge(consts, 4)
            act.wait_ge(vec_loaded, 16)
            for m in range(DC):
                act.wait_ge(x_loaded[m // 2], 16)
                norm_chunk(0, Lin(m), 0, V_FFN1)
            ffn(0, 0, 1, 1, V_MIX, U_FFN1, G_FFN1)

            norm_rms(1)
            with act.Fori(0, 4) as i:
                for e in range(2):
                    split_raw(Lin(U_MIX + 2 + e, 2, i))
            for k in range(4):
                split_raw(Lin(U_MIX + 10 + k))
            act.wait_ge(rcol_copied, 1)
            for t in range(4):
                nc.scalar.activation(v_a[:, t, :], bank[3 + t][:, :], ACT.Copy, scale=rstd_col[:, t:t + 1]).then_inc(va_ready, 1)
            for k in range(5):
                split_raw(Lin(U_MIX + 14 + k))
            split_raw(Lin(U_MIX + 19))
            act.wait_ge(bank_read, G_MIX + 13 + 2)
            vb_bank = bank[Lin(G_MIX + 13).slot]
            for t in range(4):
                ins = nc.scalar.activation(v_b[:, t, :], vb_bank[:, t * P:(t + 1) * P], ACT.Copy, scale=rstd_col[:, t:t + 1])
            ins.then_inc(bank_read, 1)

            for t in range(len(TILES) + 3):
                if t < len(TILES):
                    kind, m, j, e = TILES[t]
                    nk = tile_keys(t)
                    act.wait_ge(row_max_ready, t + 1)
                    if t >= 2:
                        act.wait_ge(transposed, t - 1)
                    r = row[:, t % 2, :]
                    if kind == "b":
                        h = m + 4 * e
                        nc.scalar.activation(r[:, 3:4], vecs[:, V_SINK + h:V_SINK + h + 1], ACT.Exp, bias=r[:, 1:2])
                    nc.scalar.activation(prob[:, t % 2, 0:nk], score[:, t % 2, 0:nk], ACT.Exp, bias=r[:, 1:2],
                                         accum_out=r[:, 2:3]).then_inc(exp_ready, 1)
                if 2 <= t < len(TILES) + 2:
                    s = t - 2
                    nk = tile_keys(s)
                    act.wait_ge(transposed, s + 1)
                    if s >= 2:
                        act.wait_ge(attended, s - 1)
                    nc.scalar.activation(prob_t[:, s % 2, 0:nk], bank[5 + s % 2][:, 0:nk], ACT.Copy).then_inc(prob_t_ready, 1)
                if t >= 3 and (t - 3) % 2 == 1:
                    s = t - 3
                    kind, m, j, e = TILES[s]
                    act.wait_ge(attended, s + 1)
                    o = bank[(s // 2) % 2][:, 0:P]
                    if kind == "a":
                        nc.scalar.activation(grid(ya_hi[:, m, :], 16 * j, 16), o.rearrange("p (r c) -> p r c", r=8), ACT.Copy)\
                          .then_inc(att_hi_ready, 1)
                    else:
                        nc.scalar.activation(yb_hi[:, m, j * P:(j + 1) * P], o, ACT.Copy).then_inc(att_hi_ready, 1)

            with act.Fori(0, DC // 2) as i:
                for e in range(2):
                    n, g = Lin(U_MERGE0 + 3 * e, 6, i), Lin(G_MERGE0 + 4 * e, 8, i)
                    for k in range(2):
                        split_raw(n + k + 2)
                        act.wait_ge(bank_read, (g + k + 3).v())
                        nc.scalar.activation(gate_sig[:, k, :], gate_pre[:, k, :], ACT.Sigmoid).then_inc(sig_ready, 1)
                    split_raw(n + 4)
                    act.wait_ge(merged_ready, Lin(e + 1, 2, i).v())
                    nc.scalar.activation(merged_hi[:, bass.ds(i * 2 + e, 1), :], merged[:, :].unsqueeze(1), ACT.Copy)\
                      .then_inc(merged_hi_ready, 1)
            with act.Fori(0, DC // 2) as i:
                for e in range(2):
                    split_raw(Lin(U_WOUT0 + 2 + e, 2, i))
                    act.wait_ge(bank_read, Lin(G_WOUT0 + e + 3, 2, i).v())
                    norm_chunk(2, Lin(e, 2, i), 2, V_FFN2)

            ffn(1, 2, 3, None, 0, U_FFN2, G_FFN2)
            norm_rms(3)
            for m in range(DC):
                act.wait_ge(x_scaled, m + 1)
                norm_chunk(4, Lin(m), 3, V_LN0)
            norm_rms(4)

            split_raw(Lin(U_GATES + 2))
            act.wait_ge(f_abs_ready, 1)
            nc.scalar.activation(g_rows[3][:, :], g_rows[2][:, :], ACT.Exp, scale=-1.0).then_inc(gates_act, 1)
            act.wait_ge(gates_act, 1)
            nc.scalar.activation(g_rows[4][:, :], g_rows[3][:, :], ACT.Ln, bias=1.0).then_inc(gates_act, 1)
            act.wait_ge(gates_dve, 3)
            nc.scalar.activation(g_rows[9][:, :], g_rows[8][:, :], ACT.Exp, scale=-1.0).then_inc(gates_act, 1)

            with act.Fori(0, M_HEADS) as i:
                n0, g0 = Lin(U_HEAD0, U_HEAD, i), Lin(G_HEAD0, G_HEAD, i)
                for c in range(4):
                    split_raw(n0 + 3 * c + 2)
                    act.wait_ge(bank_read, (g0 + 3 * c + 3).v())
                    nc.scalar.activation(xm_hi[:, c, :], xm[:, c, 3:T + 3], ACT.Copy).then_inc(xm_hi_ready, 1)
                    act.wait_ge(conv_ready, Lin(c + 1, 4, i).v())
                    nc.scalar.activation(xc[:, c, :], conv[:, :], ACT.Silu).then_inc(xc_ready, 1)
                    act.wait_ge(xc_ready, Lin(c + 1, 4, i).v())
                    nc.scalar.activation(xy_hi[:, c, :], xc[:, c, :], ACT.Copy).then_inc(xc_hi_ready, 1)
                    for k, (dst, f) in enumerate(((o_sig, ACT.Sigmoid), (z_act, ACT.Silu))):
                        split_raw(n0 + 3 * c + k + 3)
                        act.wait_ge(bank_read, (g0 + 3 * c + k + 4).v())
                        nc.scalar.activation(dst[:, c, :], pre[:, k, :], f).then_inc(oz_ready, 1)
                for si in range(4):
                    act.wait_ge(w_arg, Lin(si + 1, 4, i).v())
                    nc.scalar.activation(sw[:, si, si * P:T], sw[:, si, si * P:T], ACT.Exp).then_inc(w_exp, 1)
                for k in range(4):
                    split_raw(n0 + 14 + k)
                for t in range(4):
                    nc.scalar.activation(v_m[:, t, :], bank[3 + t][:, :], ACT.Copy).then_inc(v_m_ready, 1)
                act.wait_ge(den_ready, Lin(1, 1, i).v())
                nc.scalar.activation(den[:, :], bank[5][:, :], ACT.Abs).then_inc(den_abs, 1)
                for c in range(4):
                    act.wait_ge(h_centred, Lin(c + 1, 4, i).v())
                    if c >= 2:
                        act.wait_ge(h_squared, Lin(c - 1, 3, i).v())
                    nc.scalar.activation(sq[:, c % 2, :], hh[:, c, :], ACT.Square).then_inc(h_sq_ready, 1)
                act.wait_ge(m_stat, Lin(2, 2, i).v())
                nc.scalar.activation(den[:, :], stat[:, :], ACT.Sqrt, bias=eps[:, 0:1], scale=1.0 / M_DV).then_inc(m_rms, 1)
                for c in range(4):
                    act.wait_ge(y_ready, Lin(c + 1, 4, i).v())
                    nc.scalar.activation(xy_hi[:, c, :], hh[:, c, :], ACT.Copy).then_inc(y_hi_ready, 1)
                for k in range(4):
                    split_raw(n0 + 18 + k)

            for m in range(DC):
                if m == 0:
                    act.wait_ge(bank_read, G_PAIR0 + 2)
                norm_chunk(5, Lin(m), 4, V_LN1)
            norm_rms(5)

            act.wait_ge(rate_dve, 1)
            nc.scalar.activation(rate[:, 1, :], rate[:, 0, :], ACT.Exp, scale=-1.0).then_inc(rate_act, 1)
            act.wait_ge(rate_act, 1)
            nc.scalar.activation(rate[:, 2, :], rate[:, 1, :], ACT.Ln, bias=1.0).then_inc(rate_act, 1)
            with act.Fori(0, 4) as i:
                n0, g0 = Lin(U_PAIR0, U_PAIR, i), Lin(G_PAIR0, G_PAIR, i)
                for c in range(3):
                    split_raw(n0 + c + 2)
                    act.wait_ge(rconv_ready, Lin(c + 1, 3, i).v())
                    nc.scalar.activation(rc_hi[:, c, :], rc[:, c, :], ACT.Copy).then_inc(rc_hi_ready, 1)
                for c in range(3):
                    split_raw(n0 + c + 5)
                    act.wait_ge(bank_read, (g0 + 3 + c + 3).v())
                    nc.scalar.activation(g_act[:, c, :], g_pre[:, c % 2, :], ACT.Silu).then_inc(g_ready, 1)
                for k, dst in enumerate((rgate, igate)):
                    split_raw(n0 + 8 + k)
                    for c in range(3):
                        b = (3, 4, 5, 6, 7, 2)[3 * k + c]
                        nc.scalar.activation(dst[:, c, :], bank[b][:, :], ACT.Sigmoid, bias=pvec[:, 15 + 3 * k + c:16 + 3 * k + c])\
                          .then_inc(rgates, 1)
                act.wait_ge(rgates, Lin(3, 6, i).v())
                for c in range(3):
                    nc.scalar.activation(decay[:, c, :], rgate[:, c, :], ACT.Exp, scale=pair_rate[:, 0, c:c + 1]).then_inc(r_act, 1)
                    nc.scalar.activation(tanh[:, c, :], rgate[:, c, :], ACT.Tanh, scale=pair_rate[:, 1, c:c + 1]).then_inc(r_act, 1)
                for c in range(3):
                    act.wait_ge(b_squared, Lin(c + 1, 3, i).v())
                    nc.scalar.activation(tanh[:, c, :], tanh[:, c, :], ACT.Sqrt).then_inc(b_root, 1)
                for c in range(3):
                    act.wait_ge(ry_ready, Lin(c + 1, 3, i).v())
                    nc.scalar.activation(ry_hi[:, bass.ds(i * 3 + c, 1), :], rc[:, c, :].unsqueeze(1), ACT.Copy).then_inc(ry_hi_ready, 1)
            with act.Fori(0, DC // 2) as i:
                for e in range(2):
                    for part in range(2):
                        split_raw(Lin(U_ROUT + 2 * e + part + 2, 4, i))
                    act.wait_ge(bank_read, Lin(G_ROUT + e + 3, 2, i).v())
                    norm_chunk(6, Lin(e, 2, i), None, 0)
            norm_rms(6)

        @block.vector
        def _(dve):
            step = Steps(dve, vec_step)
            nc.vector.memset(ones[:, :], 1.0).then_inc(consts, 1)
            nc.vector.memset(eps[:, :], EPS).then_inc(consts, 1)
            nc.vector.memset(gate[:, 0:1], 0.0).then_inc(bank_read, 1)
            nc.vector.memset(gate[:, 1:2], 0.0).then_inc(bank_read, 1)
            nc.vector.memset(up[:, 0:1], 0.0).then_inc(consts, 1)
            nc.vector.memset(up[:, 1:2], 0.0).then_inc(consts, 1)

            def at_chunk(t, m):
                return t[:, bass.ds(m.v(), 1), :] if m.i is not None else t[:, m.c:m.c + 1, :]

            def split_lo(n):
                dve.wait_ge(hi_ready, (n + 1).v())
                nc.vector.tensor_tensor(w_lo[:, n.slot, :], w_raw[:, n.slot, :], w_hi[:, n.slot, :].bitcast(F32), ALU.subtract)\
                  .then_inc(lo_ready, 1)

            def lo_part(dst, src, hi):
                return nc.vector.tensor_tensor(dst, src, hi.bitcast(F32), ALU.subtract)

            def unit_done(n):
                dve.wait_ge(unit_used, (n + 1).v())

            def scaled(dst, g):
                return nc.vector.tensor_tensor(dst, bank[g.slot][:, :], rstd[:, :], ALU.mult)

            def u_lo_chunk(nu, m, gcol):
                dve.wait_ge(u_hi_ready, m.v() + 8 * nu + 1 if m.i is not None else 8 * nu + m.c + 1)
                col = vecs[:, bass.ds(m.v() + gcol, 1)] if m.i is not None else vecs[:, gcol + m.c:gcol + m.c + 1]
                nc.vector.scalar_tensor_tensor(at_chunk(u_lo, m), at_chunk(x, m), col, at_chunk(u_hi, m).bitcast(F32),
                                               ALU.mult, ALU.subtract).then_inc(u_lo_ready, 1)

            def norm_rstd(q):
                dve.wait_ge(rms_ready, q + 1)
                nc.vector.reciprocal(rstd[:, :], rms[:, :]).then_inc(rstd_ready, 1)
                dve.wait_ge(rstd_ready, q + 1)

            def add_to_x(m, g, factor):
                nc.vector.scalar_tensor_tensor(at_chunk(x, m), bank[g.slot][:, :].unsqueeze(1), factor, at_chunk(x, m),
                                               ALU.mult, ALU.add).then_inc(bank_read, 1)

            def ffn(f, q, nu_next, gcol, u0, g0):
                norm_rstd(q)
                with dve.Fori(0, F_CHUNKS) as i:
                    n, g = Lin(u0, 2, i), Lin(g0, 2, i)
                    split_lo(n + 2)
                    unit_done(n)
                    scaled(gate[:, :], g).then_inc(bank_read, 1)
                    split_lo(n + 3)
                    unit_done(n + 1)
                    scaled(up[:, :], g + 1).then_inc(bank_read, 1)
                    dve.wait_ge(gate_acted, Lin(f * F_CHUNKS + 1, 1, i).v())
                    dve.wait_ge(bank_read, (g + 4).v())
                    nc.vector.tensor_tensor(hid[:, :], gate_act[:, :], up[:, :], ALU.mult).then_inc(hid_ready, 1)
                    dve.wait_ge(hid_hi_ready, Lin(f * F_CHUNKS + 1, 1, i).v())
                    lo_part(hid_lo[:, bass.ds(i, 1), :], hid[:, :].unsqueeze(1), hid_hi[:, bass.ds(i, 1), :])\
                        .then_inc(hid_lo_ready, 1)
                with dve.Fori(0, DC // 2) as i:
                    for e in range(2):
                        n, g = Lin(u0 + 2 * F_CHUNKS + 3 * e, 6, i), Lin(g0 + 2 * F_CHUNKS + e, 2, i)
                        for part in range(3):
                            split_lo(n + part + 2)
                        unit_done(n + 2)
                        add_to_x(Lin(e, 2, i), g, 0.5)
                        if nu_next is not None:
                            u_lo_chunk(nu_next, Lin(e, 2, i), gcol)

            def convolve(dst, src, w, b, c):
                step(nc.vector.tensor_scalar(dst, src[:, c, 0:T], w(0), b, ALU.mult, ALU.add))
                for j in range(1, 4):
                    step.wait()
                    ins = nc.vector.scalar_tensor_tensor(dst, src[:, c, j:j + T], w(j), dst, ALU.mult, ALU.add)
                    if j < 3:
                        step(ins)
                return ins

            split_lo(Lin(0))
            split_lo(Lin(1))
            dve.wait_ge(vec_loaded, 16)
            for m in range(DC):
                u_lo_chunk(0, Lin(m), V_FFN1)
            ffn(0, 0, 1, V_MIX, U_FFN1, G_FFN1)

            norm_rstd(1)
            for m in range(4):
                n, g = Lin(U_MIX + m), Lin(G_MIX + m)
                split_lo(n + 2)
                unit_done(n)
                by_window = "p (r j c) -> p j r c"
                nc.vector.tensor_tensor(qk_a[:, m, :].rearrange("p (j r c) -> p j r c", j=4, r=8),
                                        bank[g.slot][:, :].rearrange(by_window, j=4, r=8),
                                        rstd[:, :].rearrange(by_window, j=4, r=8), ALU.mult).then_inc(bank_read, 1)
            with dve.Fori(0, 2) as i:
                for e in range(2):
                    n, g = Lin(U_MIX + 4 + e, 2, i), Lin(G_MIX + 4 + e, 2, i)
                    split_lo(n + 2)
                    unit_done(n)
                    nc.vector.tensor_tensor(qk_a[:, bass.ds(i * 2 + e + 4, 1), :], bank[g.slot][:, :].unsqueeze(1),
                                            rstd[:, :].unsqueeze(1), ALU.mult).then_inc(bank_read, 1)
            dve.wait_ge(rcol_ready, 1)
            nc.vector.tensor_copy(rstd_col[:, :], stat[:, 0:4]).then_inc(rcol_copied, 1)
            for k in range(4):
                split_lo(Lin(U_MIX + 10 + k))
            dve.wait_ge(tab_loaded, 32)
            for k in range(5):
                n, g = Lin(U_MIX + 12 + k), Lin(G_MIX + 8 + k)
                split_lo(n + 2)
                unit_done(n)
                scaled(unrot[:, :], g).then_inc(bank_read, 1)
                dve.wait_ge(bank_read, (g + 3).v())
                step(nc.vector.tensor_tensor(rot_cos[:, :], unrot[:, :], rope[:, 0, :], ALU.mult))
                for b in range(4):
                    s0, d0 = 32 * b, 32 * (b ^ 1)
                    step(nc.vector.tensor_tensor(rot_sin[d0:d0 + 32, :], unrot[s0:s0 + 32, :], rope[s0:s0 + 32, 1, :], ALU.mult))
                step.wait()
                nc.vector.tensor_tensor(qk_b[:, k, :], rot_cos[:, :], rot_sin[:, :], ALU.add).then_inc(rotated, 1)
            split_lo(Lin(U_MIX + 19))

            for t in range(len(TILES) + 4):
                if t < len(TILES):
                    kind, m, j, e = TILES[t]
                    nk = tile_keys(t)
                    h = 2 * m + e if kind == "a" else m + 4 * e
                    dve.wait_ge(scored, t + 1)
                    if kind == "a" and j == 0:
                        dve.wait_ge(bias_loaded[h % 2], 16 * (h // 2 + 1))
                    if kind == "a":
                        table = bias[:, h % 2, BIAS_OF[j] * 256:(BIAS_OF[j] + 1) * 256]
                    else:
                        off = 0 if j > 0 else P
                        table = mask_b[:, off:off + nk]
                    r = row[:, t % 2, :]
                    nc.vector.scalar_tensor_tensor(score[:, t % 2, 0:nk], bank[3 + t % 2][:, 0:nk], SCALE, table,
                                                   ALU.mult, ALU.add).then_inc(biased, 1)
                    dve.wait_ge(biased, t + 1)
                    step(nc.vector.reduce_max(r[:, 0:1], score[:, t % 2, 0:nk], AX_X))
                    step.wait()
                    if kind == "a":
                        nc.vector.tensor_scalar(r[:, 1:2], r[:, 0:1], -1.0, None, ALU.mult).then_inc(row_max_ready, 1)
                    else:
                        nc.vector.tensor_scalar(r[:, 1:2], r[:, 0:1], vecs[:, V_SINK + h:V_SINK + h + 1], -1.0,
                                                ALU.max, ALU.mult).then_inc(row_max_ready, 1)
                if 1 <= t < len(TILES) + 1:
                    s = t - 1
                    kind = TILES[s][0]
                    nk = tile_keys(s)
                    r = row[:, s % 2, :]
                    dve.wait_ge(exp_ready, s + 1)
                    if kind == "a":
                        step(nc.vector.reciprocal(r[:, 5:6], r[:, 2:3]))
                    else:
                        step(nc.vector.tensor_tensor(r[:, 4:5], r[:, 2:3], r[:, 3:4], ALU.add))
                        step.wait()
                        step(nc.vector.reciprocal(r[:, 5:6], r[:, 4:5]))
                    step.wait()
                    nc.vector.tensor_scalar(prob[:, s % 2, 0:nk], prob[:, s % 2, 0:nk], r[:, 5:6], None, ALU.mult)\
                      .then_inc(prob_ready, 1)
                if t >= 4 and (t - 4) % 2 == 1:
                    s = t - 4
                    kind, m, j, e = TILES[s]
                    dve.wait_ge(att_hi_ready, s // 2 + 1)
                    o = bank[(s // 2) % 2][:, 0:P]
                    if kind == "a":
                        lo_part(grid(ya_lo[:, m, :], 16 * j, 16), o.rearrange("p (r c) -> p r c", r=8),
                                grid(ya_hi[:, m, :], 16 * j, 16)).then_inc(att_lo_ready, 1)
                    else:
                        lo_part(yb_lo[:, m, j * P:(j + 1) * P], o, yb_hi[:, m, j * P:(j + 1) * P]).then_inc(att_lo_ready, 1)

            with dve.Fori(0, DC // 2) as i:
                for e in range(2):
                    n, g = Lin(U_MERGE0 + 3 * e, 6, i), Lin(G_MERGE0 + 4 * e, 8, i)
                    for k in range(2):
                        split_lo(n + k + 2)
                        unit_done(n + k)
                        scaled(gate_pre[:, k, :], g + k).then_inc(bank_read, 1)
                    split_lo(n + 4)
                    unit_done(n + 2)
                    dve.wait_ge(sig_ready, Lin(2 * e + 2, 4, i).v())
                    for k in range(2):
                        nc.vector.tensor_tensor(branch[:, k, :], bank[(g + 2 + k).slot][:, :], gate_sig[:, k, :], ALU.mult)\
                          .then_inc(bank_read, 1)
                    dve.wait_ge(bank_read, (g + 6).v())
                    nc.vector.tensor_tensor(merged[:, :], branch[:, 0, :], branch[:, 1, :], ALU.add).then_inc(merged_ready, 1)
                    dve.wait_ge(merged_hi_ready, Lin(e + 1, 2, i).v())
                    m = Lin(e, 2, i)
                    lo_part(at_chunk(merged_lo, m), merged[:, :].unsqueeze(1), at_chunk(merged_hi, m)).then_inc(merged_lo_ready, 1)
            with dve.Fori(0, DC // 2) as i:
                for e in range(2):
                    n, g = Lin(U_WOUT0 + e, 2, i), Lin(G_WOUT0 + e, 2, i)
                    split_lo(n + 2)
                    unit_done(n)
                    add_to_x(Lin(e, 2, i), g, 1.0)
                    u_lo_chunk(2, Lin(e, 2, i), V_FFN2)

            ffn(1, 2, None, 0, U_FFN2, G_FFN2)
            norm_rstd(3)
            for m in range(DC):
                nc.vector.scalar_tensor_tensor(x[:, m, :], x[:, m, :], vecs[:, V_FINAL + m:V_FINAL + m + 1], rstd[:, :],
                                               ALU.mult, ALU.mult).then_inc(x_scaled, 1)
            for m in range(DC):
                u_lo_chunk(3, Lin(m), V_LN0)
            norm_rstd(4)

            n, g = Lin(U_GATES), Lin(G_GATES)
            split_lo(n + 2)
            unit_done(n)
            gb = bank[g.slot]
            i_row, f_row, f_abs, f_exp, f_log, a_row, cum_f, neg_m, m_row, e_row = g_rows
            step(nc.vector.tensor_tensor(i_row[:, :], gb[0:4, :], rstd[0:4, :], ALU.mult))
            nc.vector.tensor_tensor(f_row[:, :], gb[32:36, :], rstd[32:36, :], ALU.mult).then_inc(bank_read, 1)
            step.wait()
            step(nc.vector.tensor_scalar(i_row[:, :], i_row[:, :], vecs[0:4, V_BIF:V_BIF + 1], None, ALU.add))
            dve.wait_ge(bank_read, G_GATES + 3)
            step(nc.vector.tensor_scalar(f_row[:, :], f_row[:, :], vecs[0:4, V_BIF + 1:V_BIF + 2], None, ALU.add))
            step.wait()
            nc.vector.scalar_tensor_tensor(f_abs[:, :], f_row[:, :], -1.0, f_row[:, :], ALU.mult, ALU.max).then_inc(f_abs_ready, 1)
            dve.wait_ge(gates_act, 2)
            step(nc.vector.scalar_tensor_tensor(f_log[:, :], f_row[:, :], 0.0, f_log[:, :], ALU.min, ALU.subtract))
            step(nc.vector.memset(f_abs[:, :], 1.0))
            step.wait()
            step(nc.vector.tensor_tensor_scan(cum_f[:, :], f_abs[:, :], f_log[:, :], 0.0, ALU.mult, ALU.add))
            step.wait()
            nc.vector.tensor_tensor(a_row[:, :], i_row[:, :], cum_f[:, :], ALU.subtract).then_inc(gates_dve, 1)
            dve.wait_ge(gates_dve, 1)
            step(nc.vector.tensor_tensor_scan(m_row[:, :], f_abs[:, :], a_row[:, :], 0.0, ALU.mult, ALU.max))
            step.wait()
            nc.vector.tensor_scalar(neg_m[:, :], m_row[:, :], -1.0, None, ALU.mult).then_inc(gates_dve, 1)
            dve.wait_ge(gates_dve, 2)
            nc.vector.tensor_tensor(m_row[:, :], cum_f[:, :], m_row[:, :], ALU.add).then_inc(gates_dve, 1)
            dve.wait_ge(gates_pe, 1)
            step(nc.vector.tensor_copy(a_col[:, :, :], bank[3][:, 0:16].rearrange("p (t h) -> p t h", t=4)))
            for b in range(8):
                dve.wait_ge(gates_pe, b + 2)
                dst = (neg_max if b < 4 else floor)[:, b % 4, :]
                nc.vector.tensor_copy(dst, bank[4 + b % 2][:, :]).then_inc(gates_dve, 1)
            for c in range(4):
                step(nc.vector.memset(xm[:, c, 0:3], 0.0))

            with dve.Fori(0, M_HEADS) as i, step.turns(i, M_HEADS, 2 + 4 * 3 + 6 + 9):
                n0, g0 = Lin(U_HEAD0, U_HEAD, i), Lin(G_HEAD0, G_HEAD, i)
                step.wait()
                step(nc.vector.tensor_copy(hvec[:, :], vecs[:, bass.ds(i * V_PER_HEAD + V_HEAD, V_PER_HEAD)]))
                step(nc.vector.tensor_copy(a_head[:, :].unsqueeze(2), a_col[:, :, bass.ds(i, 1)]))
                step.wait()
                for c in range(4):
                    split_lo(n0 + 3 * c + 2)
                    unit_done(n0 + 3 * c)
                    scaled(xm[:, c, 3:T + 3], g0 + 3 * c).then_inc(bank_read, 1)
                    dve.wait_ge(bank_read, (g0 + 3 * c + 3).v())
                    convolve(conv[:, :], xm, lambda j: hvec[:, 4 * c + j:4 * c + j + 1], hvec[:, 16 + c:17 + c], c)\
                        .then_inc(conv_ready, 1)
                    dve.wait_ge(xm_hi_ready, Lin(c + 1, 4, i).v())
                    lo_part(xm_lo[:, c, :], xm[:, c, 3:T + 3], xm_hi[:, c, :]).then_inc(xm_lo_ready, 1)
                    dve.wait_ge(xc_hi_ready, Lin(c + 1, 4, i).v())
                    lo_part(xy_lo[:, c, :], xc[:, c, :], xy_hi[:, c, :]).then_inc(xc_lo_ready, 1)
                    for k in range(2):
                        split_lo(n0 + 3 * c + k + 3)
                        unit_done(n0 + 3 * c + k + 1)
                        if c > 0:
                            dve.wait_ge(oz_ready, Lin(2 * c - 1 + k, 8, i).v())
                        scaled(pre[:, k, :], g0 + 3 * c + k + 1).then_inc(bank_read, 1)
                for si in range(4):
                    nc.vector.tensor_scalar(sw[:, si, si * P:T].unsqueeze(1), neg_max[:, bass.ds(i, 1), si * P:T],
                                            a_head[:, si:si + 1], 0.0, ALU.add, ALU.min).then_inc(w_arg, 1)
                for k in range(2):
                    split_lo(n0 + 14 + k)
                    unit_done(n0 + 12 + k)
                    for e in range(2):
                        g = g0 + 12 + 2 * k + e
                        dst = (q_m, k_m)[k][:, e, :]
                        nc.vector.tensor_scalar(dst, bank[g.slot][:, :], M_DK ** -0.5 if k == 0 else 1.0, None, ALU.mult)\
                          .then_inc(bank_read, 1)
                for k in range(2):
                    split_lo(n0 + 16 + k)
                for si in range(4):
                    dve.wait_ge(s_ready, Lin(si + 1, 4, i).v())
                    dve.wait_ge(w_masked, Lin(si + 1, 4, i).v())
                    nc.vector.tensor_tensor(sw[:, si, si * P:T], bank[3 + si % 2][:, si * P:T], sw[:, si, si * P:T], ALU.mult)\
                      .then_inc(sw_ready, 1)
                dve.wait_ge(den_abs, Lin(1, 1, i).v())
                step(nc.vector.tensor_tensor(den[:, :].unsqueeze(1), den[:, :].unsqueeze(1), floor[:, bass.ds(i, 1), :], ALU.max))
                step.wait()
                step(nc.vector.reciprocal(den[:, :], den[:, :]))
                step.wait()
                for c in range(4):
                    step(nc.vector.tensor_tensor(hh[:, c, :], o_sig[:, c, :], den[:, :], ALU.mult))
                step.wait()
                for c in range(4):
                    dve.wait_ge(num_ready, Lin(c + 1, 4, i).v())
                    nc.vector.tensor_tensor(hh[:, c, :], bank[(6, 7, 3, 4)[c]][:, :], hh[:, c, :], ALU.mult).then_inc(h_ready, 1)
                dve.wait_ge(m_stat, Lin(1, 2, i).v())
                dve.wait_ge(h_ready, Lin(4, 4, i).v())
                for c in range(4):
                    nc.vector.scalar_tensor_tensor(hh[:, c, :], stat[:, :], -1.0 / M_DV, hh[:, c, :], ALU.mult, ALU.add)\
                      .then_inc(h_centred, 1)
                dve.wait_ge(m_rms, Lin(1, 1, i).v())
                step(nc.vector.reciprocal(den[:, :], den[:, :]))
                for c in range(4):
                    step.wait()
                    step(nc.vector.scalar_tensor_tensor(hh[:, c, :], hh[:, c, :], hvec[:, 20 + c:21 + c], den[:, :],
                                                        ALU.mult, ALU.mult))
                    step.wait()
                    step(nc.vector.scalar_tensor_tensor(hh[:, c, :], xc[:, c, :], hvec[:, 24 + c:25 + c], hh[:, c, :],
                                                        ALU.mult, ALU.add))
                    step.wait()
                    nc.vector.tensor_tensor(hh[:, c, :], hh[:, c, :], z_act[:, c, :], ALU.mult).then_inc(y_ready, 1)
                    dve.wait_ge(y_hi_ready, Lin(c + 1, 4, i).v())
                    lo_part(xy_lo[:, c, :], hh[:, c, :], xy_hi[:, c, :]).then_inc(y_lo_ready, 1)
                for k in range(4):
                    split_lo(n0 + 18 + k)
                    unit_done(n0 + 16 + k)
                    for e in range(2):
                        add_to_x(Lin(2 * k + e), g0 + 16 + 2 * k + e, 1.0)

            for m in range(DC):
                u_lo_chunk(4, Lin(m), V_LN1)
            norm_rstd(5)

            lam = vecs[:, V_PAIR:V_ALL].rearrange("p (a b) -> p a b", b=V_PER_PAIR)[:, :, 21:24]
            rates = [rate[:, k, :].rearrange("p (a b) -> p a b", b=3) for k in range(5)]
            nc.vector.scalar_tensor_tensor(rates[0], lam, -1.0, lam, ALU.mult, ALU.max).then_inc(rate_dve, 1)
            step(nc.vector.tensor_scalar(rates[3], lam, -1.0, 0.0, ALU.mult, ALU.max))
            dve.wait_ge(rate_act, 2)
            step.wait()
            step(nc.vector.tensor_tensor(rates[2], rates[3], rates[2], ALU.add))
            step.wait()
            step(nc.vector.tensor_scalar(rates[3], rates[2], -LRU_C, None, ALU.mult))
            step(nc.vector.tensor_scalar(rates[4], rates[2], LRU_C, None, ALU.mult))
            for c in range(3):
                step(nc.vector.memset(xr[:, c, 0:3], 0.0))
            with dve.Fori(0, 4) as i, step.turns(i, 4, 2 + 3 * 3 + 3 * 4):
                n0, g0 = Lin(U_PAIR0, U_PAIR, i), Lin(G_PAIR0, G_PAIR, i)
                step.wait()
                step(nc.vector.tensor_copy(pvec[:, :], vecs[:, bass.ds(i * V_PER_PAIR + V_PAIR, V_PER_PAIR)]))
                step(nc.vector.tensor_copy(pair_rate[:, :, :], rate[:, 3:5, bass.ds(i * 3, 3)]))
                step.wait()
                for c in range(3):
                    split_lo(n0 + c + 2)
                    unit_done(n0 + c)
                    scaled(xr[:, c, 3:T + 3], g0 + c).then_inc(bank_read, 1)
                    dve.wait_ge(bank_read, (g0 + c + 3).v())
                    convolve(rc[:, c, :], xr, lambda j: pvec[:, 4 * c + j:4 * c + j + 1], pvec[:, 12 + c:13 + c], c)\
                        .then_inc(rconv_ready, 1)
                    dve.wait_ge(rc_hi_ready, Lin(c + 1, 3, i).v())
                    lo_part(rc_lo[:, c, :], rc[:, c, :], rc_hi[:, c, :]).then_inc(rc_lo_ready, 1)
                for c in range(3):
                    split_lo(n0 + c + 5)
                    unit_done(n0 + 3 + c)
                    if c == 2:
                        dve.wait_ge(g_ready, Lin(1, 3, i).v())
                    scaled(g_pre[:, c % 2, :], g0 + 3 + c).then_inc(bank_read, 1)
                for k in range(2):
                    split_lo(n0 + 8 + k)
                for c in range(3):
                    dve.wait_ge(r_act, Lin(2 * c + 2, 6, i).v())
                    step(nc.vector.tensor_tensor(igate[:, c, :], igate[:, c, :], rc[:, c, :], ALU.mult))
                    step(nc.vector.tensor_tensor(rgate[:, c, :], decay[:, c, :], decay[:, c, :], ALU.mult))
                    step.wait()
                    nc.vector.scalar_tensor_tensor(tanh[:, c, :], rgate[:, c, :], 1.0, tanh[:, c, :], ALU.add, ALU.mult)\
                        .then_inc(b_squared, 1)
                for c in range(3):
                    dve.wait_ge(b_root, Lin(c + 1, 3, i).v())
                    step(nc.vector.tensor_tensor(igate[:, c, :], tanh[:, c, :], igate[:, c, :], ALU.mult))
                    step.wait()
                    step(nc.vector.tensor_tensor_scan(rgate[:, c, :], decay[:, c, :], igate[:, c, :], 0.0, ALU.mult, ALU.add))
                    step.wait()
                    nc.vector.tensor_tensor(rc[:, c, :], rgate[:, c, :], g_act[:, c, :], ALU.mult).then_inc(ry_ready, 1)
                    dve.wait_ge(ry_hi_ready, Lin(c + 1, 3, i).v())
                    lo_part(ry_lo[:, bass.ds(i * 3 + c, 1), :], rc[:, c, :].unsqueeze(1), ry_hi[:, bass.ds(i * 3 + c, 1), :])\
                        .then_inc(ry_lo_ready, 1)
            with dve.Fori(0, DC // 2) as i:
                for e in range(2):
                    n, g = Lin(U_ROUT + 2 * e, 4, i), Lin(G_ROUT + e, 2, i)
                    for part in range(2):
                        split_lo(n + part + 2)
                    unit_done(n + 1)
                    add_to_x(Lin(e, 2, i), g, 1.0)
            norm_rstd(6)
            for m in range(DC):
                nc.vector.scalar_tensor_tensor(x[:, m, :], x[:, m, :], vecs[:, V_FINAL2 + m:V_FINAL2 + m + 1], rstd[:, :],
                                               ALU.mult, ALU.mult).then_inc(out_ready, 1)

        @block.gpsimd
        def _(pool):
            step = Steps(pool, pool_step)

            def norm_sum(q):
                if q > 0:
                    pool.wait_ge(stat_ready, q)
                nc.gpsimd.memset(sumsq[:, :], 0.0).then_inc(sq_added, 1)
                for m in range(DC):
                    pool.wait_ge(sq_ready, DC * q + m + 1)
                    pool.wait_ge(sq_added, 9 * q + m + 1)
                    nc.gpsimd.tensor_tensor(sumsq[:, :], sumsq[:, :], sq[:, m % 2, :], ALU.add).then_inc(sq_added, 1)

            norm_sum(0)
            norm_sum(1)
            pool.wait_ge(stat_ready, 2)
            pool.dma_start(rope[:, :, :], rope_in).then_inc(tab_loaded, 16)
            pool.dma_start(mask_b[:, :], maskb_in).then_inc(tab_loaded, 16)
            for h in range(2):
                pool.dma_start(bias[:, h, :], bias_in[h]).then_inc(bias_loaded[h], 16)
            pool.wait_ge(va_ready, 4)
            for j in range(4):
                for b in range(2):
                    for r in range(4):
                        p0 = (r % 2) * 64 + KEY_COL0[j]
                        pool.dma_start(v_win[32 * r:32 * r + 32, j, b, :], v_a[p0:p0 + 32, 2 * b + r // 2, :])\
                            .then_inc(v_moved, 16)
            for h in range(2, 8):
                pool.wait_ge(biased, 8 * (h // 2))
                pool.dma_start(bias[:, h % 2, :], bias_in[h]).then_inc(bias_loaded[h % 2], 16)
            for q in range(2, 4):
                norm_sum(q)
            pool.wait_ge(stat_ready, 4)
            pool.dma_start(sel[:, :, :], sel_in).then_inc(sel_loaded, 16)
            pool.dma_start(causal[:, :], causal_in).then_inc(causal_loaded, 16)
            norm_sum(4)

            pool.wait_ge(causal_loaded, 16)
            with pool.Fori(0, M_HEADS) as i, step.turns(i, M_HEADS, 2):
                for si in range(4):
                    pool.wait_ge(w_exp, Lin(si + 1, 4, i).v())
                    dia = sw[:, si, si * P:(si + 1) * P]
                    nc.gpsimd.tensor_tensor(dia, dia, causal[:, :], ALU.mult).then_inc(w_masked, 1)
                pool.wait_ge(h_ready, Lin(2, 4, i).v())
                step(nc.gpsimd.tensor_tensor(hsum[:, :], hh[:, 0, :], hh[:, 1, :], ALU.add))
                pool.wait_ge(h_ready, Lin(3, 4, i).v())
                step.wait()
                step(nc.gpsimd.tensor_tensor(hsum[:, :], hsum[:, :], hh[:, 2, :], ALU.add))
                pool.wait_ge(h_ready, Lin(4, 4, i).v())
                step.wait()
                nc.gpsimd.tensor_tensor(hsum[:, :], hsum[:, :], hh[:, 3, :], ALU.add).then_inc(h_summed, 1)
                for c in range(1, 4):
                    pool.wait_ge(h_sq_ready, Lin(c + 1, 4, i).v())
                    if c > 1:
                        pool.wait_ge(h_squared, Lin(c - 1, 3, i).v())
                    nc.gpsimd.tensor_tensor(hsum[:, :], sq[:, 0, :] if c == 1 else hsum[:, :], sq[:, c % 2, :], ALU.add)\
                        .then_inc(h_squared, 1)
            pool.wait_ge(m_stat, 2 * M_HEADS)
            norm_sum(5)
            norm_sum(6)


def blocks(w, pairs):
    import numpy as np
    u = np.zeros((P, UB * P), np.float32)
    for k, (r, c) in enumerate(pairs):
        u[:, k * P:(k + 1) * P] = w[r * P:(r + 1) * P, c * P:(c + 1) * P]
    return u


def wide(w, r0):
    import numpy as np
    return np.concatenate([w[r0 * P:(r0 + 1) * P], w[(r0 + 1) * P:(r0 + 2) * P]], axis=1)


def weight_stream(a):
    import numpy as np
    units = []

    def columns(w, c, rows=range(8)):
        units.append(blocks(w, [(r, c) for r in rows]))

    def ffn(gate_w, up_w, down_w):
        for c in range(F_CHUNKS):
            columns(gate_w, c)
            columns(up_w, c)
        for c in range(DC):
            for part in range(3):
                columns(down_w, c, range(8 * part, min(8 * part + 8, F_CHUNKS)))

    order = np.concatenate([np.arange(HD * h, HD * (h + 1)) for j in range(4) for h in (j, j + 4)])
    ffn(a["ffn1_w_gate"][0], a["ffn1_w_up"][0], a["ffn1_w_down"][0])
    w = a["w_in"][0]
    for c in range(8):
        columns(w, c)
    for part in range(4):
        units.append(wide(w[:, 1024:1536], 2 * part))
    qb = w[:, 1536:2048][:, order]
    for c in range(4):
        columns(qb, c)
    columns(w, 16)
    columns(w, 17)
    wb = a["w_branch_b"][0][order]
    for c in range(DC):
        columns(w, 18 + c)
        columns(w, 26 + c)
        units.append(np.concatenate([blocks(a["w_branch_a"][0], [(r, c) for r in range(4)])[:, :4 * P],
                                     blocks(wb, [(r, c) for r in range(4)])[:, :4 * P]], axis=1))
    for c in range(DC):
        columns(a["w_out"][0], c)
    ffn(a["ffn2_w_gate"][0], a["ffn2_w_up"][0], a["ffn2_w_down"][0])

    w = a["m_w_in_2"][0]
    gates = np.zeros((D, P), np.float32)
    gates[:, 0:4] = w[:, 6144:6148]
    gates[:, 32:36] = w[:, 6148:6152]
    columns(gates, 0)
    for h in range(M_HEADS):
        for c in range(4):
            for base in (0, 32, 16):
                columns(w, base + 4 * h + c)
        for wk in (a["m_w_q_2"][0, h], a["m_w_k_2"][0, h]):
            units.append(blocks(wk, [(r, e) for e in range(2) for r in range(4)]))
        for part in range(2):
            units.append(wide(a["m_w_v_2"][0, h], 2 * part))
        for k in range(4):
            units.append(blocks(a["m_w_out_2"][0], [(4 * h + r, 2 * k + e) for e in range(2) for r in range(4)]))
    w = a["r_w_in_2"][0]
    for p in range(4):
        for base in (0, 12):
            for c in range(3):
                columns(w, base + 3 * p + c)
        for wg in (a["r_w_a_2"][0], a["r_w_x_2"][0]):
            pair = np.zeros((3 * P, 3 * P), np.float32)
            pair[0:192, 0:192] = wg[2 * p]
            pair[192:384, 192:384] = wg[2 * p + 1]
            units.append(blocks(pair, GATE_BLOCKS))
    for c in range(DC):
        for part in range(2):
            columns(a["r_w_out_2"][0], c, range(6 * part, 6 * part + 6))
    while len(units) < U_ALL:
        units.append(np.zeros((P, UB * P), np.float32))
    assert len(units) == U_ALL
    return np.stack(units)


def vectors(a):
    import numpy as np
    v = np.zeros((P, V_ALL), np.float32)

    def put(col, vec):
        v[:, col:col + len(vec) // P] = vec.reshape(-1, P).T

    for col, vec in ((V_FFN1, a["ffn1_norm"][0]), (V_MIX, a["mix_norm"][0]), (V_FFN2, a["ffn2_norm"][0]),
                     (V_FINAL, a["final_norm"]), (V_LN0, a["ln_g_2"][0]), (V_LN1, a["ln_g_2"][1]),
                     (V_FINAL2, a["final_g_2"])):
        put(col, vec)
    v[:, V_SINK:V_SINK + 8] = a["sink_logit"][0][None, :]
    v[0:4, V_BIF] = a["m_b_i_2"][0]
    v[0:4, V_BIF + 1] = a["m_b_f_2"][0]
    for h in range(M_HEADS):
        col, part = V_HEAD + h * V_PER_HEAD, slice(h * M_DV, (h + 1) * M_DV)
        for c in range(4):
            for j in range(4):
                put(col + 4 * c + j, a["m_conv_w_2"][0, j, part][c * P:(c + 1) * P])
        put(col + 16, a["m_conv_b_2"][0, part])
        put(col + 20, a["m_norm_w_2"][0, part])
        put(col + 24, a["m_skip_2"][0, part])
    for p in range(4):
        col, part = V_PAIR + p * V_PER_PAIR, slice(p * 3 * P, (p + 1) * 3 * P)
        for c in range(3):
            for j in range(4):
                put(col + 4 * c + j, a["r_conv_w_2"][0, j, part][c * P:(c + 1) * P])
        for k, name in enumerate(("r_conv_b_2", "r_b_a_2", "r_b_x_2", "r_lam_2")):
            put(col + 12 + 3 * k, a[name][0, part])
    return v


def neighbourhood_bias(rpb):
    import numpy as np
    out = np.full((8, P, 3, 256), -1e30, np.float32)
    for kind, j in enumerate((0, 1, 3)):
        for c in range(16):
            col = 16 * j + c
            start = min(max(col - 8, 0), 64 - 16)
            k0 = start - KEY_COL0[j]
            for r in range(8):
                for i in range(8):
                    out[:, r * 16 + c, kind, i * 32 + k0:i * 32 + k0 + 16] = \
                        rpb[:, i - r + 7, start - col + 15:start - col + 31]
    return out.reshape(8, P, 768)


def tables():
    import numpy as np
    half = HD // 2
    inv = np.float32(10000.0) ** (-np.arange(half, dtype=np.float32) / np.float32(half))
    ang = (np.arange(T, dtype=np.float32)[None, :] * inv[:, None].astype(np.float32)).astype(np.float32)
    cos, sin = np.cos(ang).astype(np.float32), np.sin(ang).astype(np.float32)
    rope = np.stack([np.tile(cos, (4, 1)), np.concatenate([sin, -sin, sin, -sin])], axis=1)
    q, k = np.arange(P)[:, None], np.arange(P)[None, :]
    far = np.float32(-1e30)
    mask = np.concatenate([np.where(k >= q, 0, far), np.zeros((P, P)), np.where(k <= q, 0, far)], axis=1).astype(np.float32)
    sel = np.zeros((4, M_HEADS, P), np.float32)
    for h in range(M_HEADS):
        sel[h, h, :] = 1
    return rope.astype(np.float32), mask, np.eye(P, dtype=np.float32), sel, np.where(k >= q, 1, 0).astype(np.float32)


def kernel(**inputs):
    import numpy as np
    import concourse.bacc as bacc
    from concourse.bass_utils import run_bass_kernel_spmd

    a = {k: np.asarray(v) for k, v in inputs.items()}
    rope, mask, ident, sel, causal = tables()
    arrays = {
        "x_t": np.ascontiguousarray(a["x"][0].T),
        "weights": weight_stream(a),
        "vectors": vectors(a),
        "neighbour_bias": neighbourhood_bias(a["na_rpb"][0]),
        "rope_table": rope, "band_mask": mask, "identity": ident, "head_rows": sel, "causal_mask": causal,
    }
    nc = bacc.Bacc("TRN2", target_bir_lowering=False, num_devices=1)
    args = [nc.dram_tensor(n, v.shape, F32, kind="ExternalInput").ap() for n, v in arrays.items()]
    out = nc.dram_tensor("out_t", (D, T), F32, kind="ExternalOutput").ap()
    build_program(nc, *args, out)
    got = run_bass_kernel_spmd(nc, [arrays], core_ids=[0]).results[0]["out_t"]
    return np.ascontiguousarray(got.T)[None]
```

```python
from contextlib import ExitStack, contextmanager

import concourse.bass as bass
from concourse import mybir

F32 = mybir.dt.float32
F32R = mybir.dt.float32r
ACT = mybir.ActivationFunctionType
ALU = mybir.AluOpType
AX_X = mybir.AxisListType.X

P = 128
T = 512
D = 1024
DC = D // P
UB = 8
F_CHUNKS = 22
HD = 64
SCALE = HD ** -0.5
EPS = 1e-6
LRU_C = 8.0
M_HEADS = 4
M_DV = 512
M_DK = 256
RG_CHUNKS = 12
KEY_COL0 = (0, 8, 24, 32)
BIAS_OF = (0, 1, 1, 2)

U_FFN = 2 * F_CHUNKS + 3 * DC
U_QKV = 18
U_MERGE = 3 * DC
U_WOUT = DC
U_HEAD = 20
U_PAIR = 8
U_FFN1 = 0
U_MIX = U_FFN1 + U_FFN
U_MERGE0 = U_MIX + U_QKV
U_WOUT0 = U_MERGE0 + U_MERGE
U_FFN2 = U_WOUT0 + U_WOUT
U_GATES = U_FFN2 + U_FFN
U_HEAD0 = U_GATES + 1
U_PAIR0 = U_HEAD0 + M_HEADS * U_HEAD
U_ROUT = U_PAIR0 + 4 * U_PAIR
U_END = U_ROUT + 2 * DC
U_ALL = U_END + 3

G_FFN = 2 * F_CHUNKS + DC
G_FFN1 = 0
G_MIX = G_FFN1 + G_FFN
G_MERGE0 = G_MIX + 14
G_WOUT0 = G_MERGE0 + 4 * DC
G_FFN2 = G_WOUT0 + DC
G_GATES = G_FFN2 + G_FFN
G_HEAD0 = G_GATES + 1
G_HEAD = 24
G_PAIR0 = G_HEAD0 + M_HEADS * G_HEAD
G_PAIR = 6
G_ROUT = G_PAIR0 + 4 * G_PAIR

V_BANKS = (5, 6, 7, 2)
OUT_BANKS = (G_HEAD0 % 2, 1 - G_HEAD0 % 2, 6, 7)

V_FFN1, V_MIX, V_FFN2, V_FINAL, V_LN0, V_LN1, V_FINAL2 = (8 * k for k in range(7))
V_SINK = 56
V_BIF = 64
V_HEAD = 66
V_PER_HEAD = 28
V_PAIR = V_HEAD + M_HEADS * V_PER_HEAD
V_PER_PAIR = 24
V_ALL = V_PAIR + 4 * V_PER_PAIR

GATE_BLOCKS = [(0, 0), (1, 0), (0, 1), (1, 1), (2, 1), (1, 2), (2, 2)]


class Lin:

    def __init__(self, c, m=0, i=None):
        self.c, self.m, self.i = c, m, i

    def __add__(self, k):
        return Lin(self.c + k, self.m, self.i)

    def v(self, scale=1):
        return self.c * scale if self.i is None else self.i * (self.m * scale) + self.c * scale

    def half(self):
        return Lin(self.c // 2, self.m // 2, self.i)

    @property
    def slot(self):
        assert self.m % 2 == 0
        return self.c % 2


def of_head(i):
    return (lambda c, m: Lin(c, m, i)) if i is not None else (lambda c, m: Lin(c + m * (M_HEADS - 1)))


class Steps:

    def __init__(self, engine, sem):
        self.engine, self.sem, self.at = engine, sem, Lin(0)

    def __call__(self, ins):
        ins.then_inc(self.sem, 1)
        self.at = self.at + 1

    def wait(self):
        self.engine.wait_ge(self.sem, self.at.v())

    @contextmanager
    def turns(self, i, n, per):
        start = self.at.c
        self.at = Lin(start, per, i)
        yield
        assert self.at.c - start == per, (self.at.c - start, per)
        self.at = Lin(start + n * per)


def build_program(nc, x_in, w_in, vec_in, bias_in, rope_in, maskb_in, ident_in, sel_in, causal_in, out):
    ctx = ExitStack()
    with ctx:
        def sb(name, shape, dt=F32, scope=ctx):
            return scope.enter_context(nc.sbuf_tensor(name, shape, dt))

        def sem(name):
            return ctx.enter_context(nc.semaphore(name))

        x = sb("x", [P, DC, T])
        rstd = sb("rstd", [P, T])
        rms = sb("rms", [P, T])
        sq = sb("sq", [P, 2, T])
        sumsq = sb("sumsq", [P, T])
        w_raw = sb("w_raw", [P, 2, UB * P])
        w_hi = sb("w_hi", [P, 2, UB * P], F32R)
        w_lo = sb("w_lo", [P, 2, UB * P], F32R)
        u_hi = sb("u_hi", [P, DC, T], F32R)
        u_lo = sb("u_lo", [P, DC, T], F32R)
        vecs = sb("vecs", [P, V_ALL])
        ones = sb("ones", [P, P])
        ident = sb("ident", [P, P])
        eps = sb("eps", [P, 1])

        with ExitStack() as s:
            hid_hi = sb("hid_hi", [P, F_CHUNKS, T], F32R, s)
            hid_lo = sb("hid_lo", [P, F_CHUNKS, T], F32R, s)
            gate = sb("gate", [P, T], F32, s)
            gate_act = sb("gate_act", [P, T], F32, s)
            up = sb("up", [P, T], F32, s)
            hid = sb("hid", [P, T], F32, s)

        with ExitStack() as s:
            ya_hi = sb("ya_hi", [P, 4, T], F32R, s)
            ya_lo = sb("ya_lo", [P, 4, T], F32R, s)
            yb_hi = sb("yb_hi", [P, 4, T], F32R, s)
            yb_lo = sb("yb_lo", [P, 4, T], F32R, s)
            with ExitStack() as s2:
                qk_a = sb("qk_a", [P, 8, T], F32, s2)
                v_a = sb("v_a", [P, 4, T], F32, s2)
                v_win = sb("v_win", [P, 4, 2, T], F32, s2)
                qk_b = sb("qk_b", [P, 5, T], F32, s2)
                v_b = sb("v_b", [P, 4, P], F32, s2)
                bias = sb("bias", [P, 2, 3 * 256], F32, s2)
                rope = sb("rope", [P, 2, T], F32, s2)
                mask_b = sb("mask_b", [P, 3 * P], F32, s2)
                rstd_col = sb("rstd_col", [P, 4], F32, s2)
                unrot = sb("unrot", [P, T], F32, s2)
                rot_cos = sb("rot_cos", [P, T], F32, s2)
                rot_sin = sb("rot_sin", [P, T], F32, s2)
                score = sb("score", [P, 2, 384], F32, s2)
                prob = sb("prob", [P, 2, 384], F32, s2)
                prob_t = sb("prob_t", [P, 2, 384], F32, s2)
                row = sb("row", [P, 2, 8], F32, s2)
            with ExitStack() as s2:
                merged_hi = sb("merged_hi", [P, DC, T], F32R, s2)
                merged_lo = sb("merged_lo", [P, DC, T], F32R, s2)
                gate_pre = sb("gate_pre", [P, 2, T], F32, s2)
                gate_sig = sb("gate_sig", [P, 2, T], F32, s2)
                branch = sb("branch", [P, 2, T], F32, s2)
                merged = sb("merged", [P, T], F32, s2)

        with ExitStack() as s:
            neg_max = sb("neg_max", [P, M_HEADS, T], F32, s)
            floor = sb("floor", [P, M_HEADS, T], F32, s)
            a_col = sb("a_col", [P, 4, 4], F32, s)
            a_head = sb("a_head", [P, 4], F32, s)
            hvec = sb("hvec", [P, V_PER_HEAD], F32, s)
            sel = sb("sel", [4, M_HEADS, P], F32, s)
            causal = sb("causal", [P, P], F32, s)
            xm = sb("xm", [P, 4, T + 3], F32, s)
            xm_hi = sb("xm_hi", [P, 4, T], F32R, s)
            xm_lo = sb("xm_lo", [P, 4, T], F32R, s)
            with ExitStack() as s2:
                g_rows = [sb(f"g_row{k}", [4, T], F32, s2) for k in range(10)]
            xc = sb("xc", [P, 4, T], F32, s)
            xy_hi = sb("xy_hi", [P, 4, T], F32R, s)
            xy_lo = sb("xy_lo", [P, 4, T], F32R, s)
            o_sig = sb("o_sig", [P, 4, T], F32, s)
            z_act = sb("z_act", [P, 4, T], F32, s)
            q_m = sb("q_m", [P, 2, T], F32, s)
            k_m = sb("k_m", [P, 2, T], F32, s)
            v_m = sb("v_m", [P, 4, T], F32, s)
            sw = sb("sw", [P, 4, T], F32, s)
            pre = sb("pre", [P, 2, T], F32, s)
            conv = sb("conv", [P, T], F32, s)
            den = sb("den", [P, T], F32, s)
            hsum = sumsq
            hh = sb("hh", [P, 4, T], F32, s)

        with ExitStack() as s:
            ry_hi = sb("ry_hi", [P, RG_CHUNKS, T], F32R, s)
            ry_lo = sb("ry_lo", [P, RG_CHUNKS, T], F32R, s)
            xr = sb("xr", [P, 3, T + 3], F32, s)
            rc = sb("rc", [P, 3, T], F32, s)
            rc_hi = sb("rc_hi", [P, 3, T], F32R, s)
            rc_lo = sb("rc_lo", [P, 3, T], F32R, s)
            g_pre = sb("g_pre", [P, 2, T], F32, s)
            g_act = sb("g_act", [P, 3, T], F32, s)
            rgate = sb("rgate", [P, 3, T], F32, s)
            igate = sb("igate", [P, 3, T], F32, s)
            decay = sb("decay", [P, 3, T], F32, s)
            tanh = sb("tanh", [P, 3, T], F32, s)
            pvec = sb("pvec", [P, V_PER_PAIR], F32, s)
            rate = sb("rate", [P, 5, RG_CHUNKS], F32, s)
            pair_rate = sb("pair_rate", [P, 2, 3], F32, s)

        bank = [ctx.enter_context(nc.psum_tensor(f"bank{k}", [P, T], F32)) for k in range(8)]
        stat = bank[2]

        x_loaded = [sem(f"x_loaded{k}") for k in range(4)]
        vec_loaded = sem("vec_loaded")
        tab_loaded = sem("tab_loaded")
        ident_loaded = sem("ident_loaded")
        sel_loaded = sem("sel_loaded")
        causal_loaded = sem("causal_loaded")
        consts = sem("consts")
        raw_loaded = [sem("raw_loaded0"), sem("raw_loaded1")]
        hi_ready = sem("hi_ready")
        lo_ready = sem("lo_ready")
        unit_used = sem("unit_used")
        bank_read = sem("bank_read")
        sq_ready = sem("sq_ready")
        sq_added = sem("sq_added")
        stat_ready = sem("stat_ready")
        rms_ready = sem("rms_ready")
        rstd_ready = sem("rstd_ready")
        u_hi_ready = sem("u_hi_ready")
        u_lo_ready = sem("u_lo_ready")
        x_scaled = sem("x_scaled")
        gate_acted = sem("gate_acted")
        hid_ready = sem("hid_ready")
        hid_hi_ready = sem("hid_hi_ready")
        hid_lo_ready = sem("hid_lo_ready")
        rcol_ready = sem("rcol_ready")
        rcol_copied = sem("rcol_copied")
        va_ready = sem("va_ready")
        v_moved = sem("v_moved")
        cos_ready = sem("cos_ready")
        rotated = sem("rotated")
        bias_loaded = [sem("bias_loaded0"), sem("bias_loaded1")]
        scored = sem("scored")
        biased = sem("biased")
        row_max_ready = sem("row_max_ready")
        exp_ready = sem("exp_ready")
        prob_ready = sem("prob_ready")
        transposed = sem("transposed")
        prob_t_ready = sem("prob_t_ready")
        attended = sem("attended")
        att_hi_ready = sem("att_hi_ready")
        att_lo_ready = sem("att_lo_ready")
        sig_ready = sem("sig_ready")
        merged_ready = sem("merged_ready")
        merged_hi_ready = sem("merged_hi_ready")
        merged_lo_ready = sem("merged_lo_ready")
        f_abs_ready = sem("f_abs_ready")
        gates_dve = sem("gates_dve")
        gates_act = sem("gates_act")
        gates_pe = sem("gates_pe")
        xm_hi_ready = sem("xm_hi_ready")
        xm_lo_ready = sem("xm_lo_ready")
        conv_ready = sem("conv_ready")
        xc_ready = sem("xc_ready")
        xc_hi_ready = sem("xc_hi_ready")
        xc_lo_ready = sem("xc_lo_ready")
        oz_ready = sem("oz_ready")
        v_m_ready = sem("v_m_ready")
        w_arg = sem("w_arg")
        w_exp = sem("w_exp")
        w_masked = sem("w_masked")
        s_ready = sem("s_ready")
        sw_ready = sem("sw_ready")
        den_ready = sem("den_ready")
        den_abs = sem("den_abs")
        num_ready = sem("num_ready")
        h_ready = sem("h_ready")
        h_summed = sem("h_summed")
        m_stat = sem("m_stat")
        h_centred = sem("h_centred")
        h_squared = sem("h_squared")
        h_sq_ready = sem("h_sq_ready")
        m_rms = sem("m_rms")
        y_ready = sem("y_ready")
        y_hi_ready = sem("y_hi_ready")
        y_lo_ready = sem("y_lo_ready")
        rate_dve = sem("rate_dve")
        rate_act = sem("rate_act")
        rconv_ready = sem("rconv_ready")
        rc_hi_ready = sem("rc_hi_ready")
        rc_lo_ready = sem("rc_lo_ready")
        g_ready = sem("g_ready")
        rgates = sem("rgates")
        r_act = sem("r_act")
        b_squared = sem("b_squared")
        b_root = sem("b_root")
        ry_ready = sem("ry_ready")
        ix_ready = sem("ix_ready")
        a_squared = sem("a_squared")
        h_scanned = sem("h_scanned")
        ry_hi_ready = sem("ry_hi_ready")
        ry_lo_ready = sem("ry_lo_ready")
        vec_step = sem("vec_step")
        pool_step = sem("pool_step")
        out_ready = sem("out_ready")
        stored = sem("stored")

        block = ctx.enter_context(nc.Block())

        def grid(ap, c0, n):
            return ap.rearrange("p (r c) -> p r c", r=8)[:, :, c0:c0 + n]

        A_TILES = [("a", m, j, e) for m in range(4) for j in range(4) for e in range(2)]
        B_TILES = [("b", m, n, e) for m in range(4) for n in range(4) for e in range(2)]
        TILES = A_TILES + B_TILES

        def key_blocks(n):
            return [b for b in (n - 1, n, n + 1) if 0 <= b < 4]

        def tile_keys(t):
            kind, m, j, e = TILES[t]
            return 256 if kind == "a" else P * len(key_blocks(j))

        @block.sync
        def _(sp):
            for k in range(2):
                sp.dma_start(w_raw[:, k, :], w_in[k]).then_inc(raw_loaded[k], 16)
            with sp.Fori(1, U_ALL // 2) as i:
                for k in range(2):
                    sp.wait_ge(lo_ready, i * 2 + (k - 1))
                    sp.dma_start(w_raw[:, k, :], w_in[bass.ds(i * 2 + k, 1)].rearrange("a p c -> (a p) c"))\
                      .then_inc(raw_loaded[k], 16)
            for m in range(DC):
                sp.wait_ge(out_ready, m + 1)
                sp.dma_start(out[m * P:(m + 1) * P, :], x[:, m, :]).then_inc(stored, 16)
            sp.wait_ge(stored, 16 * DC)

        @block.tensor
        def _(pe):
            def product(o, pairs, n, last_of_unit=False, start=True, stop=True):
                ins = None
                for k, (b, hi, lo) in enumerate(pairs):
                    wh = w_hi[:, n.slot, b * P:(b + 1) * P]
                    wl = w_lo[:, n.slot, b * P:(b + 1) * P]
                    nc.tensor.matmul(o, wh, hi, start=start and k == 0, stop=False)
                    nc.tensor.matmul(o, wh, lo, start=False, stop=False)
                    ins = nc.tensor.matmul(o, wl, hi, start=False, stop=stop and k == len(pairs) - 1)
                if last_of_unit:
                    ins.then_inc(unit_used, 1)
                return ins

            def unit_ready(n):
                pe.wait_ge(lo_ready, (n + 1).v())

            def bank_free(g):
                pe.wait_ge(bank_read, (g + 1).v())

            def linear8(n, g):
                unit_ready(n)
                bank_free(g)
                product(bank[g.slot][:, :], [(k, u_hi[:, k, :], u_lo[:, k, :]) for k in range(8)], n, True)

            def first_unit(n, g, nu):
                unit_ready(n)
                bank_free(g)
                for k in range(DC):
                    pe.wait_ge(u_lo_ready, DC * nu + k + 1)
                    product(bank[g.slot][:, :], [(k, u_hi[:, k, :], u_lo[:, k, :])], n, k == DC - 1,
                            start=k == 0, stop=k == DC - 1)

            def norm_stat(q):
                pe.wait_ge(sq_added, 9 * (q + 1))
                if q == 0:
                    pe.wait_ge(consts, 4)
                nc.tensor.matmul(stat[:, :], ones[:, :], sumsq[:, :], start=True, stop=True).then_inc(stat_ready, 1)

            def ffn(f, q, nu, u0, g0):
                first_unit(Lin(u0), Lin(g0), nu)
                norm_stat(q)
                linear8(Lin(u0 + 1), Lin(g0 + 1))
                with pe.Fori(1, F_CHUNKS) as i:
                    n, g = Lin(u0, 2, i), Lin(g0, 2, i)
                    linear8(n, g)
                    linear8(n + 1, g + 1)
                pe.wait_ge(hid_lo_ready, F_CHUNKS * (f + 1))
                with pe.Fori(0, DC // 2) as i:
                    for e in range(2):
                        n, g = Lin(u0 + 2 * F_CHUNKS + 3 * e, 6, i), Lin(g0 + 2 * F_CHUNKS + e, 2, i)
                        bank_free(g)
                        for part in range(3):
                            unit_ready(n + part)
                            ks = range(8 * part, min(8 * part + 8, F_CHUNKS))
                            product(bank[g.slot][:, :], [(k - 8 * part, hid_hi[:, k, :], hid_lo[:, k, :]) for k in ks],
                                    n + part, True, start=part == 0, stop=part == 2)

            ffn(0, 0, 0, U_FFN1, G_FFN1)

            first_unit(Lin(U_MIX), Lin(G_MIX), 1)
            norm_stat(1)
            linear8(Lin(U_MIX + 1), Lin(G_MIX + 1))
            with pe.Fori(1, 4) as i:
                for e in range(2):
                    linear8(Lin(U_MIX + e, 2, i), Lin(G_MIX + e, 2, i))
            pe.wait_ge(rstd_ready, 2)
            for t in range(4):
                ins = nc.tensor.matmul(stat[:, t:t + 1], rstd[0:1, t * P:(t + 1) * P], ones[0:1, 0:1], start=True, stop=True)
            ins.then_inc(rcol_ready, 1)
            for part in range(4):
                n = Lin(U_MIX + 8 + part)
                unit_ready(n)
                for t in range(4):
                    tok = slice(t * P, (t + 1) * P)
                    for c in range(2):
                        k = 2 * part + c
                        wh, wl = w_hi[:, n.slot, c * T:(c + 1) * T], w_lo[:, n.slot, c * T:(c + 1) * T]
                        nc.tensor.matmul(bank[3 + t][:, :], u_hi[:, k, tok], wh, start=k == 0, stop=False)
                        nc.tensor.matmul(bank[3 + t][:, :], u_lo[:, k, tok], wh, start=False, stop=False)
                        ins = nc.tensor.matmul(bank[3 + t][:, :], u_hi[:, k, tok], wl, start=False, stop=k == 7)
                ins.then_inc(unit_used, 1)
            for k in range(5):
                linear8(Lin(U_MIX + 12 + k), Lin(G_MIX + 8 + k))
            n, g = Lin(U_MIX + 17), Lin(G_MIX + 13)
            unit_ready(n)
            bank_free(g)
            for t in range(4):
                tok = slice(t * P, (t + 1) * P)
                for k in range(8):
                    wh, wl = w_hi[:, n.slot, k * P:(k + 1) * P], w_lo[:, n.slot, k * P:(k + 1) * P]
                    o = bank[g.slot][:, tok]
                    nc.tensor.matmul(o, u_hi[:, k, tok], wh, start=k == 0, stop=False)
                    nc.tensor.matmul(o, u_lo[:, k, tok], wh, start=False, stop=False)
                    ins = nc.tensor.matmul(o, u_hi[:, k, tok], wl, start=False, stop=k == 7)
            ins.then_inc(unit_used, 1)

            pe.wait_ge(bank_read, G_MIX + 14 + 2)
            pe.wait_ge(va_ready, 4)
            pe.wait_ge(rotated, 5)
            pe.wait_ge(ident_loaded, 16)
            for t in range(len(TILES) + 3):
                if t < len(TILES):
                    kind, m, j, e = TILES[t]
                    half = slice(HD * e, HD * (e + 1))
                    if t >= 2:
                        pe.wait_ge(biased, t - 1)
                    o = bank[3 + t % 2][:, 0:tile_keys(t)]
                    if kind == "a":
                        q_t, k_t = qk_a[half, m, j * P:(j + 1) * P], grid(qk_a[half, 4 + m, :], KEY_COL0[j], 32)
                    else:
                        kb = key_blocks(j)
                        q_t = qk_b[half, m, j * P:(j + 1) * P]
                        k_t = qk_b[half, 4, kb[0] * P:(kb[-1] + 1) * P]
                    nc.tensor.matmul(o, q_t, k_t, start=True, stop=True).then_inc(scored, 1)
                if 2 <= t < len(TILES) + 2:
                    s = t - 2
                    pe.wait_ge(prob_ready, s + 1)
                    if s >= 2:
                        pe.wait_ge(prob_t_ready, s - 1)
                    for b in range(tile_keys(s) // P):
                        ins = nc.tensor.transpose(bank[5 + s % 2][:, b * P:(b + 1) * P], prob[:, s % 2, b * P:(b + 1) * P],
                                                  ident[:, :])
                    ins.then_inc(transposed, 1)
                if t >= 3:
                    s = t - 3
                    kind, m, j, e = TILES[s]
                    pe.wait_ge(prob_t_ready, s + 1)
                    if s == 0:
                        pe.wait_ge(v_moved, 16 * 16)
                    if e == 0 and s >= 4:
                        pe.wait_ge(att_lo_ready, s // 2 - 1)
                    o = bank[(s // 2) % 2][HD * e:HD * (e + 1), 0:P]
                    nb = tile_keys(s) // P
                    for b in range(nb):
                        if kind == "a":
                            h = 2 * m + e
                            v_t = v_win[:, j, b, h * HD:(h + 1) * HD]
                        else:
                            v_t = v_b[:, key_blocks(j)[b], e * HD:(e + 1) * HD]
                        ins = nc.tensor.matmul(o, v_t, prob_t[:, s % 2, b * P:(b + 1) * P], start=b == 0, stop=b == nb - 1)
                    ins.then_inc(attended, 1)

            pe.wait_ge(att_lo_ready, len(TILES) // 2)
            with pe.Fori(0, DC // 2) as i:
                for e in range(2):
                    n, g = Lin(U_MERGE0 + 3 * e, 6, i), Lin(G_MERGE0 + 4 * e, 8, i)
                    for k in range(2):
                        unit_ready(n + k)
                        pe.wait_ge(bank_read, (g + (k - 1)).v())
                        product(bank[k][:, :], [(c, u_hi[:, c, :], u_lo[:, c, :]) for c in range(8)], n + k, True)
                    unit_ready(n + 2)
                    pe.wait_ge(bank_read, (g + 1).v())
                    product(bank[3][:, :], [(k, ya_hi[:, k, :], ya_lo[:, k, :]) for k in range(4)], n + 2)
                    product(bank[4][:, :], [(4 + k, yb_hi[:, k, :], yb_lo[:, k, :]) for k in range(4)], n + 2, True)
            pe.wait_ge(merged_lo_ready, DC)
            with pe.Fori(0, DC // 2) as i:
                for e in range(2):
                    n, g = Lin(U_WOUT0 + e, 2, i), Lin(G_WOUT0 + e, 2, i)
                    unit_ready(n)
                    bank_free(g)
                    product(bank[g.slot][:, :], [(k, merged_hi[:, k, :], merged_lo[:, k, :]) for k in range(8)], n, True)

            ffn(1, 2, 2, U_FFN2, G_FFN2)
            norm_stat(3)

            first_unit(Lin(U_GATES), Lin(G_GATES), 3)
            norm_stat(4)
            h0, gh0 = Lin(U_HEAD0), Lin(G_HEAD0)
            linear8(h0, gh0)
            linear8(h0 + 1, gh0 + 1)
            pe.wait_ge(gates_dve, 1)
            pe.wait_ge(sel_loaded, 16)
            for t in range(4):
                ins = nc.tensor.matmul(bank[3][:, 4 * t:4 * t + 4], g_rows[5][:, t * P:(t + 1) * P], ident[0:4, 0:4],
                                       start=True, stop=True)
            ins.then_inc(gates_pe, 1)
            pe.wait_ge(gates_dve, 2)
            for k, row_t in enumerate((g_rows[7], g_rows[9])):
                if k == 1:
                    pe.wait_ge(gates_act, 3)
                for h in range(M_HEADS):
                    b = 4 * k + h
                    if k == 1:
                        pe.wait_ge(gates_dve, b)
                    nc.tensor.matmul(bank[4 + h][:, :], sel[:, h, :], row_t[:, :], start=True, stop=True)\
                      .then_inc(gates_pe, 1)
                linear8(h0 + 2 + k, gh0 + 2 + k)

            def head(i):
                of = of_head(i)
                n0, g0 = of(U_HEAD0, U_HEAD), of(G_HEAD0, G_HEAD)
                for k in range(4, 6):
                    linear8(n0 + k, g0 + k)
                pe.wait_ge(xc_lo_ready, of(4, 4).v())
                for k in range(2):
                    n, g = n0 + 6 + k, g0 + 6 + 2 * k
                    unit_ready(n)
                    for e in range(2):
                        bank_free(g + e)
                        product(bank[(g + e).slot][:, :], [(4 * e + c, xy_hi[:, c, :], xy_lo[:, c, :]) for c in range(4)],
                                n, e == 1)
                linear8(n0 + 8, g0 + 10)
                pe.wait_ge(bank_read, (g0 + 10 + 2).v())
                for si in range(4):
                    if si >= 2:
                        pe.wait_ge(sw_ready, of(si - 1, 4).v())
                    for e in range(2):
                        ins = nc.tensor.matmul(bank[3 + si % 2][:, si * P:T], k_m[:, e, si * P:(si + 1) * P],
                                               q_m[:, e, si * P:T], start=e == 0, stop=e == 1)
                    ins.then_inc(s_ready, 1)
                for part in range(2):
                    n = n0 + 9 + part
                    unit_ready(n)
                    for t in range(4):
                        tok = slice(t * P, (t + 1) * P)
                        for c in range(2):
                            k = 2 * part + c
                            wh, wl = w_hi[:, n.slot, c * T:(c + 1) * T], w_lo[:, n.slot, c * T:(c + 1) * T]
                            o = bank[V_BANKS[t]][:, :]
                            nc.tensor.matmul(o, xm_hi[:, k, tok], wh, start=k == 0, stop=False)
                            nc.tensor.matmul(o, xm_lo[:, k, tok], wh, start=False, stop=False)
                            ins = nc.tensor.matmul(o, xm_hi[:, k, tok], wl, start=False, stop=k == 3)
                    ins.then_inc(unit_used, 1)
                linear8(n0 + 11, g0 + 11)
                pe.wait_ge(sw_ready, of(4, 4).v())
                pe.wait_ge(v_m_ready, of(4, 4).v())
                for si in range(4):
                    ins = nc.tensor.matmul(bank[3][:, si * P:T], ones[:, :], sw[:, si, si * P:T], start=si == 0, stop=si == 3)
                ins.then_inc(den_ready, 1)
                for c in range(4):
                    for si in range(4):
                        ins = nc.tensor.matmul(bank[4 + c][:, si * P:T], v_m[:, si, c * P:(c + 1) * P],
                                               sw[:, si, si * P:T], start=si == 0, stop=si == 3)
                    ins.then_inc(num_ready, 1)
                linear8(n0 + 12, g0 + 12)
                pe.wait_ge(h_summed, of(1, 1).v())
                nc.tensor.matmul(stat[:, :], ones[:, :], hsum[:, :], start=True, stop=True).then_inc(m_stat, 1)
                linear8(n0 + 13, g0 + 13)
                linear8(n0 + 14, g0 + 14)
                pe.wait_ge(h_squared, of(3, 3).v())
                nc.tensor.matmul(stat[:, :], ones[:, :], hsum[:, :], start=True, stop=True).then_inc(m_stat, 1)
                linear8(n0 + 15, g0 + 15)
                n_out, g_out = n0 + 16, g0 + 16
                if i is not None:
                    for k in range(4):
                        linear8(n0 + 16 + k, g0 + 16 + k)
                    n_out, g_out = n0 + 20, g0 + 20
                for k in range(4):
                    n = n_out + k
                    unit_ready(n)
                    for e in range(2):
                        j = 2 * k + e
                        g = g_out + j
                        if j < 2:
                            bank_free(g)
                        elif j >= 4:
                            pe.wait_ge(bank_read, (g + (-1)).v())
                        if j == 0:
                            pe.wait_ge(y_lo_ready, of(4, 4).v())
                        product(bank[OUT_BANKS[j % 4]][:, :], [(4 * e + c, xy_hi[:, c, :], xy_lo[:, c, :]) for c in range(4)],
                                n, e == 1)

            with pe.Fori(0, M_HEADS - 1) as i:
                head(i)
            head(None)

            def pair(n0, g0, k3, done):
                for k in range(done, 6):
                    linear8(n0 + k, g0 + k)
                pe.wait_ge(rc_lo_ready, (k3 + 3).v())
                for k in range(2):
                    n = n0 + 6 + k
                    unit_ready(n)
                    for c in range(3):
                        b = (3, 4, 5, 6, 7, 2)[3 * k + c]
                        pairs = [(s, rc_hi[:, ci, :], rc_lo[:, ci, :]) for s, (ci, co) in enumerate(GATE_BLOCKS) if co == c]
                        product(bank[b][:, :], pairs, n, c == 2)

            first_unit(Lin(U_PAIR0), Lin(G_PAIR0), 4)
            norm_stat(5)
            pair(Lin(U_PAIR0), Lin(G_PAIR0), Lin(0), 1)
            with pe.Fori(0, 3) as i:
                pair(Lin(U_PAIR0 + U_PAIR, U_PAIR, i), Lin(G_PAIR0 + G_PAIR, G_PAIR, i), Lin(3, 3, i), 0)
            pe.wait_ge(rgates, 24)
            pe.wait_ge(ry_lo_ready, 6)
            pe.wait_ge(bank_read, G_ROUT + 2)
            for part in range(2):
                if part == 1:
                    pe.wait_ge(ry_lo_ready, RG_CHUNKS)
                for m in range(DC):
                    n = Lin(U_ROUT + DC * part + m)
                    unit_ready(n)
                    product(bank[m][:, :], [(k, ry_hi[:, 6 * part + k, :], ry_lo[:, 6 * part + k, :]) for k in range(6)],
                            n, True, start=part == 0, stop=part == 1)
            pe.wait_ge(bank_read, G_ROUT + DC + 2)
            norm_stat(6)

        @block.scalar
        def _(act):
            for k in range(4):
                act.dma_start(x[:, 2 * k:2 * k + 2, :],
                              x_in[2 * k * P:(2 * k + 2) * P, :].rearrange("(c p) t -> p c t", p=P)).then_inc(x_loaded[k], 16)
                if k == 0:
                    act.dma_start(vecs[:, :], vec_in).then_inc(vec_loaded, 16)
            act.dma_start(ident[:, :], ident_in).then_inc(ident_loaded, 16)

            def split_raw(n):
                act.wait_ge(raw_loaded[n.slot], (n.half() + 1).v(16))
                if n.i is not None or n.c >= 2:
                    act.wait_ge(unit_used, (n + (-1)).v())
                nc.scalar.activation(w_hi[:, n.slot, :], w_raw[:, n.slot, :], ACT.Copy).then_inc(hi_ready, 1)

            def norm_chunk(q, m, nu, gcol):
                act.wait_ge(sq_added, m.v() + 9 * q if m.i is not None else 9 * q + m.c)
                if nu is not None:
                    col = vecs[:, bass.ds(m.v() + gcol, 1)] if m.i is not None else vecs[:, gcol + m.c:gcol + m.c + 1]
                    nc.scalar.activation(at_chunk(u_hi, m), at_chunk(x, m), ACT.Copy, scale=col).then_inc(u_hi_ready, 1)
                nc.scalar.activation(sq[:, m.slot:m.slot + 1, :], at_chunk(x, m), ACT.Square).then_inc(sq_ready, 1)

            def at_chunk(t, m):
                return t[:, bass.ds(m.v(), 1), :] if m.i is not None else t[:, m.c:m.c + 1, :]

            def norm_rms(q):
                act.wait_ge(stat_ready, q + 1)
                nc.scalar.activation(rms[:, :], stat[:, :], ACT.Sqrt, bias=eps[:, 0:1], scale=1.0 / D).then_inc(rms_ready, 1)

            def ffn(f, q, q_next, nu_next, gcol, u0, g0):
                norm_rms(q)
                act.preload_act_table(ACT.Silu)
                with act.Fori(0, F_CHUNKS) as i:
                    n, g = Lin(u0, 2, i), Lin(g0, 2, i)
                    split_raw(n + 2)
                    act.wait_ge(bank_read, (g + 3).v())
                    nc.scalar.activation(gate_act[:, :], gate[:, :], ACT.Silu).then_inc(gate_acted, 1)
                    split_raw(n + 3)
                    act.wait_ge(hid_ready, Lin(f * F_CHUNKS + 1, 1, i).v())
                    nc.scalar.activation(hid_hi[:, bass.ds(i, 1), :], hid[:, :].unsqueeze(1), ACT.Copy).then_inc(hid_hi_ready, 1)
                with act.Fori(0, DC // 2) as i:
                    for e in range(2):
                        n, g = Lin(u0 + 2 * F_CHUNKS + 3 * e, 6, i), Lin(g0 + 2 * F_CHUNKS + e, 2, i)
                        for part in range(3):
                            split_raw(n + part + 2)
                        act.wait_ge(bank_read, (g + 3).v())
                        norm_chunk(q_next, Lin(e, 2, i), nu_next, gcol)

            split_raw(Lin(0))
            split_raw(Lin(1))
            act.wait_ge(consts, 4)
            act.wait_ge(vec_loaded, 16)
            for m in range(DC):
                act.wait_ge(x_loaded[m // 2], 16)
                norm_chunk(0, Lin(m), 0, V_FFN1)
            ffn(0, 0, 1, 1, V_MIX, U_FFN1, G_FFN1)

            norm_rms(1)
            with act.Fori(0, 4) as i:
                for e in range(2):
                    split_raw(Lin(U_MIX + 2 + e, 2, i))
            for k in range(4):
                split_raw(Lin(U_MIX + 10 + k))
            act.wait_ge(rcol_copied, 1)
            for t in range(4):
                nc.scalar.activation(v_a[:, t, :], bank[3 + t][:, :], ACT.Copy, scale=rstd_col[:, t:t + 1]).then_inc(va_ready, 1)
            for k in range(5):
                split_raw(Lin(U_MIX + 14 + k))
            split_raw(Lin(U_MIX + 19))
            act.wait_ge(bank_read, G_MIX + 13 + 2)
            vb_bank = bank[Lin(G_MIX + 13).slot]
            for t in range(4):
                ins = nc.scalar.activation(v_b[:, t, :], vb_bank[:, t * P:(t + 1) * P], ACT.Copy, scale=rstd_col[:, t:t + 1])
            ins.then_inc(bank_read, 1)

            for t in range(len(TILES) + 3):
                if t < len(TILES):
                    kind, m, j, e = TILES[t]
                    nk = tile_keys(t)
                    act.wait_ge(row_max_ready, t + 1)
                    if t >= 2:
                        act.wait_ge(transposed, t - 1)
                    r = row[:, t % 2, :]
                    if kind == "b":
                        h = m + 4 * e
                        nc.scalar.activation(r[:, 3:4], vecs[:, V_SINK + h:V_SINK + h + 1], ACT.Exp, bias=r[:, 1:2])
                    nc.scalar.activation(prob[:, t % 2, 0:nk], score[:, t % 2, 0:nk], ACT.Exp, bias=r[:, 1:2],
                                         accum_out=r[:, 2:3]).then_inc(exp_ready, 1)
                if 2 <= t < len(TILES) + 2:
                    s = t - 2
                    nk = tile_keys(s)
                    act.wait_ge(transposed, s + 1)
                    if s >= 2:
                        act.wait_ge(attended, s - 1)
                    nc.scalar.activation(prob_t[:, s % 2, 0:nk], bank[5 + s % 2][:, 0:nk], ACT.Copy).then_inc(prob_t_ready, 1)
                if t >= 3 and (t - 3) % 2 == 1:
                    s = t - 3
                    kind, m, j, e = TILES[s]
                    act.wait_ge(attended, s + 1)
                    o = bank[(s // 2) % 2][:, 0:P]
                    if kind == "a":
                        nc.scalar.activation(grid(ya_hi[:, m, :], 16 * j, 16), o.rearrange("p (r c) -> p r c", r=8), ACT.Copy)\
                          .then_inc(att_hi_ready, 1)
                    else:
                        nc.scalar.activation(yb_hi[:, m, j * P:(j + 1) * P], o, ACT.Copy).then_inc(att_hi_ready, 1)

            act.preload_act_table(ACT.Sigmoid)
            with act.Fori(0, DC // 2) as i:
                for e in range(2):
                    n, g = Lin(U_MERGE0 + 3 * e, 6, i), Lin(G_MERGE0 + 4 * e, 8, i)
                    for k in range(2):
                        split_raw(n + k + 2)
                        act.wait_ge(bank_read, (g + k + 3).v())
                        nc.scalar.activation(gate_sig[:, k, :], gate_pre[:, k, :], ACT.Sigmoid).then_inc(sig_ready, 1)
                    split_raw(n + 4)
                    act.wait_ge(merged_ready, Lin(e + 1, 2, i).v())
                    nc.scalar.activation(merged_hi[:, bass.ds(i * 2 + e, 1), :], merged[:, :].unsqueeze(1), ACT.Copy)\
                      .then_inc(merged_hi_ready, 1)
            with act.Fori(0, DC // 2) as i:
                for e in range(2):
                    split_raw(Lin(U_WOUT0 + 2 + e, 2, i))
                    act.wait_ge(bank_read, Lin(G_WOUT0 + e + 3, 2, i).v())
                    norm_chunk(2, Lin(e, 2, i), 2, V_FFN2)

            ffn(1, 2, 3, None, 0, U_FFN2, G_FFN2)
            norm_rms(3)
            for m in range(DC):
                act.wait_ge(x_scaled, m + 1)
                norm_chunk(4, Lin(m), 3, V_LN0)
            norm_rms(4)

            split_raw(Lin(U_GATES + 2))
            act.wait_ge(f_abs_ready, 1)
            nc.scalar.activation(g_rows[3][:, :], g_rows[2][:, :], ACT.Exp, scale=-1.0).then_inc(gates_act, 1)
            act.wait_ge(gates_act, 1)
            nc.scalar.activation(g_rows[4][:, :], g_rows[3][:, :], ACT.Ln, bias=1.0).then_inc(gates_act, 1)
            def inner_hi(n, g, c):
                split_raw(n + 2)
                act.wait_ge(bank_read, (g + 3).v())
                nc.scalar.activation(xm_hi[:, c, :], xm[:, c, 3:T + 3], ACT.Copy).then_inc(xm_hi_ready, 1)

            def conv_act(of, h, c):
                act.wait_ge(conv_ready, of(4 * h + c + 1, 4).v())
                nc.scalar.activation(xc[:, c, :], conv[:, :], ACT.Silu).then_inc(xc_ready, 1)

            def first(c, m):
                return Lin(c)

            h0, gh0 = Lin(U_HEAD0), Lin(G_HEAD0)
            inner_hi(h0, gh0, 0)
            act.wait_ge(gates_dve, 3)
            nc.scalar.activation(g_rows[9][:, :], g_rows[8][:, :], ACT.Exp, scale=-1.0).then_inc(gates_act, 1)
            for c in range(1, 4):
                inner_hi(h0 + c, gh0 + c, c)
                conv_act(first, 0, c - 1)
            conv_act(first, 0, 3)

            def head(i):
                of = of_head(i)
                n0, g0 = of(U_HEAD0, U_HEAD), of(G_HEAD0, G_HEAD)
                def gate_act_of(j, n, g):
                    split_raw(n + 2)
                    act.wait_ge(bank_read, (g + 3).v())
                    dst, f = (o_sig, ACT.Sigmoid) if j < 4 else (z_act, ACT.Silu)
                    nc.scalar.activation(dst[:, j % 4, :], pre[:, j % 2, :], f).then_inc(oz_ready, 1)

                act.wait_ge(unit_used, (n0 + 4).v())
                act.wait_ge(xc_ready, of(4, 4).v())
                for c in range(4):
                    nc.scalar.activation(xy_hi[:, c, :], xc[:, c, :], ACT.Copy).then_inc(xc_hi_ready, 1)
                gate_act_of(0, n0 + 4, g0 + 4)
                gate_act_of(1, n0 + 5, g0 + 5)
                for si in range(4):
                    act.wait_ge(w_arg, of(si + 1, 4).v())
                    nc.scalar.activation(sw[:, si, si * P:T], sw[:, si, si * P:T], ACT.Exp).then_inc(w_exp, 1)
                split_raw(n0 + 8)
                split_raw(n0 + 9)
                gate_act_of(2, n0 + 8, g0 + 10)
                split_raw(n0 + 11)
                split_raw(n0 + 12)
                act.wait_ge(unit_used, (n0 + 11).v())
                for t in range(4):
                    nc.scalar.activation(v_m[:, t, :], bank[V_BANKS[t]][:, :], ACT.Copy).then_inc(v_m_ready, 1)
                gate_act_of(3, n0 + 11, g0 + 11)
                act.wait_ge(den_ready, of(1, 1).v())
                nc.scalar.activation(den[:, :], bank[3][:, :], ACT.Abs).then_inc(den_abs, 1)
                gate_act_of(4, n0 + 12, g0 + 12)
                gate_act_of(5, n0 + 13, g0 + 13)
                for c in range(4):
                    act.wait_ge(h_centred, of(c + 1, 4).v())
                    if c >= 2:
                        act.wait_ge(h_squared, of(c - 1, 3).v())
                    nc.scalar.activation(sq[:, c % 2, :], hh[:, c, :], ACT.Square).then_inc(h_sq_ready, 1)
                gate_act_of(6, n0 + 14, g0 + 14)
                act.wait_ge(m_stat, of(2, 2).v())
                nc.scalar.activation(den[:, :], stat[:, :], ACT.Sqrt, bias=eps[:, 0:1], scale=1.0 / M_DV).then_inc(m_rms, 1)
                gate_act_of(7, n0 + 15, g0 + 15)
                def y_hi(c):
                    act.wait_ge(y_ready, of(c + 1, 4).v())
                    nc.scalar.activation(xy_hi[:, c, :], hh[:, c, :], ACT.Copy).then_inc(y_hi_ready, 1)

                y_hi(0)
                y_hi(1)
                if i is not None:
                    inner_hi(n0 + 16, g0 + 16, 0)
                y_hi(2)
                y_hi(3)
                if i is not None:
                    for c in range(1, 4):
                        inner_hi(n0 + 16 + c, g0 + 16 + c, c)
                        if c >= 2:
                            conv_act(of, 1, c - 2)
                    for k in range(4):
                        split_raw(n0 + 22 + k)
                        if k < 2:
                            conv_act(of, 1, k + 2)
                else:
                    for k in range(4):
                        split_raw(n0 + 18 + k)
                        for m in range(2 * k, 2 * k + 2):
                            act.wait_ge(bank_read, (g0 + 16 + m + 3).v())
                            norm_chunk(5, Lin(m), 4, V_LN1)

            with act.Fori(0, M_HEADS - 1) as i:
                head(i)
            head(None)

            norm_rms(5)

            act.wait_ge(rate_dve, 1)
            nc.scalar.activation(rate[:, 1, :], rate[:, 0, :], ACT.Exp, scale=-1.0).then_inc(rate_act, 1)
            act.wait_ge(rate_act, 1)
            nc.scalar.activation(rate[:, 2, :], rate[:, 1, :], ACT.Ln, bias=1.0).then_inc(rate_act, 1)
            def pair(n0, g0, k3, k6, before):
                for c in range(3):
                    split_raw(n0 + c + 2)
                    act.wait_ge(rconv_ready, (k3 + (c + 1)).v())
                    nc.scalar.activation(rc_hi[:, c, :], rc[:, c, :], ACT.Copy).then_inc(rc_hi_ready, 1)
                if before is not None:
                    for c in range(3):
                        act.wait_ge(b_squared, (before * 3 + (c + 1)))
                        nc.scalar.activation(tanh[:, c, :], tanh[:, c, :], ACT.Sqrt).then_inc(b_root, 1)
                for c in range(3):
                    split_raw(n0 + c + 5)
                    if before is not None:
                        act.wait_ge(ry_ready, (before * 3 + (c + 1)))
                        nc.scalar.activation(ry_hi[:, bass.ds(before * 3 + c, 1), :], tanh[:, c:c + 1, :], ACT.Copy)\
                          .then_inc(ry_hi_ready, 1)
                    act.wait_ge(bank_read, (g0 + 3 + c + 3).v())
                    nc.scalar.activation(g_act[:, c, :], g_pre[:, c % 2, :], ACT.Silu).then_inc(g_ready, 1)
                for k, dst in enumerate((rgate, igate)):
                    split_raw(n0 + 8 + k)
                    for c in range(3):
                        b = (3, 4, 5, 6, 7, 2)[3 * k + c]
                        nc.scalar.activation(dst[:, c, :], bank[b][:, :], ACT.Sigmoid, bias=pvec[:, 15 + 3 * k + c:16 + 3 * k + c])\
                          .then_inc(rgates, 1)
                act.wait_ge(rgates, (k6 + 3).v())
                if before is not None:
                    act.wait_ge(ry_lo_ready, k3.v())
                for c in range(3):
                    nc.scalar.activation(decay[:, c, :], rgate[:, c, :], ACT.Exp, scale=pair_rate[:, 0, c:c + 1]).then_inc(r_act, 1)
                    nc.scalar.activation(tanh[:, c, :], rgate[:, c, :], ACT.Tanh, scale=pair_rate[:, 1, c:c + 1]).then_inc(r_act, 1)

            pair(Lin(U_PAIR0), Lin(G_PAIR0), Lin(0), Lin(0), None)
            with act.Fori(0, 3) as i:
                pair(Lin(U_PAIR0 + U_PAIR, U_PAIR, i), Lin(G_PAIR0 + G_PAIR, G_PAIR, i), Lin(3, 3, i), Lin(6, 6, i), i)
            for c in range(3):
                act.wait_ge(b_squared, 9 + c + 1)
                nc.scalar.activation(tanh[:, c, :], tanh[:, c, :], ACT.Sqrt).then_inc(b_root, 1)
            for c in range(3):
                act.wait_ge(ry_ready, 9 + c + 1)
                nc.scalar.activation(ry_hi[:, 9 + c, :], tanh[:, c, :], ACT.Copy).then_inc(ry_hi_ready, 1)
            for k in range(2 * DC):
                split_raw(Lin(U_ROUT + 2 + k))
                if k >= DC:
                    m = k - DC
                    act.wait_ge(bank_read, G_ROUT + m + 3)
                    norm_chunk(6, Lin(m), None, 0)
            norm_rms(6)

        @block.vector
        def _(dve):
            step = Steps(dve, vec_step)
            nc.vector.memset(ones[:, :], 1.0).then_inc(consts, 1)
            nc.vector.memset(eps[:, :], EPS).then_inc(consts, 1)
            nc.vector.memset(gate[:, 0:1], 0.0).then_inc(bank_read, 1)
            nc.vector.memset(gate[:, 1:2], 0.0).then_inc(bank_read, 1)
            nc.vector.memset(up[:, 0:1], 0.0).then_inc(consts, 1)
            nc.vector.memset(up[:, 1:2], 0.0).then_inc(consts, 1)

            def at_chunk(t, m):
                return t[:, bass.ds(m.v(), 1), :] if m.i is not None else t[:, m.c:m.c + 1, :]

            def split_lo(n):
                dve.wait_ge(hi_ready, (n + 1).v())
                nc.vector.tensor_tensor(w_lo[:, n.slot, :], w_raw[:, n.slot, :], w_hi[:, n.slot, :].bitcast(F32), ALU.subtract)\
                  .then_inc(lo_ready, 1)

            def lo_part(dst, src, hi):
                return nc.vector.tensor_tensor(dst, src, hi.bitcast(F32), ALU.subtract)

            def unit_done(n):
                dve.wait_ge(unit_used, (n + 1).v())

            def scaled(dst, g):
                return nc.vector.tensor_tensor(dst, bank[g.slot][:, :], rstd[:, :], ALU.mult)

            def u_lo_chunk(nu, m, gcol):
                dve.wait_ge(u_hi_ready, m.v() + 8 * nu + 1 if m.i is not None else 8 * nu + m.c + 1)
                col = vecs[:, bass.ds(m.v() + gcol, 1)] if m.i is not None else vecs[:, gcol + m.c:gcol + m.c + 1]
                nc.vector.scalar_tensor_tensor(at_chunk(u_lo, m), at_chunk(x, m), col, at_chunk(u_hi, m).bitcast(F32),
                                               ALU.mult, ALU.subtract).then_inc(u_lo_ready, 1)

            def norm_rstd(q):
                dve.wait_ge(rms_ready, q + 1)
                nc.vector.reciprocal(rstd[:, :], rms[:, :]).then_inc(rstd_ready, 1)
                dve.wait_ge(rstd_ready, q + 1)

            def add_to_x(m, g, factor, b=None):
                nc.vector.scalar_tensor_tensor(at_chunk(x, m), bank[g.slot if b is None else b][:, :].unsqueeze(1), factor, at_chunk(x, m),
                                               ALU.mult, ALU.add).then_inc(bank_read, 1)

            def ffn(f, q, nu_next, gcol, u0, g0):
                norm_rstd(q)
                with dve.Fori(0, F_CHUNKS) as i:
                    n, g = Lin(u0, 2, i), Lin(g0, 2, i)
                    split_lo(n + 2)
                    unit_done(n)
                    scaled(gate[:, :], g).then_inc(bank_read, 1)
                    split_lo(n + 3)
                    unit_done(n + 1)
                    scaled(up[:, :], g + 1).then_inc(bank_read, 1)
                    dve.wait_ge(gate_acted, Lin(f * F_CHUNKS + 1, 1, i).v())
                    dve.wait_ge(bank_read, (g + 4).v())
                    nc.vector.tensor_tensor(hid[:, :], gate_act[:, :], up[:, :], ALU.mult).then_inc(hid_ready, 1)
                    dve.wait_ge(hid_hi_ready, Lin(f * F_CHUNKS + 1, 1, i).v())
                    lo_part(hid_lo[:, bass.ds(i, 1), :], hid[:, :].unsqueeze(1), hid_hi[:, bass.ds(i, 1), :])\
                        .then_inc(hid_lo_ready, 1)
                with dve.Fori(0, DC // 2) as i:
                    for e in range(2):
                        n, g = Lin(u0 + 2 * F_CHUNKS + 3 * e, 6, i), Lin(g0 + 2 * F_CHUNKS + e, 2, i)
                        for part in range(3):
                            split_lo(n + part + 2)
                        unit_done(n + 2)
                        add_to_x(Lin(e, 2, i), g, 0.5)
                        if nu_next is not None:
                            u_lo_chunk(nu_next, Lin(e, 2, i), gcol)

            def convolve(dst, src, w, b, c):
                step(nc.vector.tensor_scalar(dst, src[:, c, 0:T], w(0), b, ALU.mult, ALU.add))
                for j in range(1, 4):
                    step.wait()
                    ins = nc.vector.scalar_tensor_tensor(dst, src[:, c, j:j + T], w(j), dst, ALU.mult, ALU.add)
                    if j < 3:
                        step(ins)
                return ins

            split_lo(Lin(0))
            split_lo(Lin(1))
            dve.wait_ge(vec_loaded, 16)
            for m in range(DC):
                u_lo_chunk(0, Lin(m), V_FFN1)
            ffn(0, 0, 1, V_MIX, U_FFN1, G_FFN1)

            norm_rstd(1)
            for m in range(4):
                n, g = Lin(U_MIX + m), Lin(G_MIX + m)
                split_lo(n + 2)
                unit_done(n)
                by_window = "p (r j c) -> p j r c"
                nc.vector.tensor_tensor(qk_a[:, m, :].rearrange("p (j r c) -> p j r c", j=4, r=8),
                                        bank[g.slot][:, :].rearrange(by_window, j=4, r=8),
                                        rstd[:, :].rearrange(by_window, j=4, r=8), ALU.mult).then_inc(bank_read, 1)
            with dve.Fori(0, 2) as i:
                for e in range(2):
                    n, g = Lin(U_MIX + 4 + e, 2, i), Lin(G_MIX + 4 + e, 2, i)
                    split_lo(n + 2)
                    unit_done(n)
                    nc.vector.tensor_tensor(qk_a[:, bass.ds(i * 2 + e + 4, 1), :], bank[g.slot][:, :].unsqueeze(1),
                                            rstd[:, :].unsqueeze(1), ALU.mult).then_inc(bank_read, 1)
            dve.wait_ge(rcol_ready, 1)
            nc.vector.tensor_copy(rstd_col[:, :], stat[:, 0:4]).then_inc(rcol_copied, 1)
            for k in range(4):
                split_lo(Lin(U_MIX + 10 + k))
            dve.wait_ge(tab_loaded, 32)
            for k in range(5):
                n, g = Lin(U_MIX + 12 + k), Lin(G_MIX + 8 + k)
                split_lo(n + 2)
                unit_done(n)
                scaled(unrot[:, :], g).then_inc(bank_read, 1)
                dve.wait_ge(bank_read, (g + 3).v())
                for b in range(4):
                    s0, d0 = 32 * b, 32 * (b ^ 1)
                    step(nc.vector.tensor_tensor(rot_sin[d0:d0 + 32, :], unrot[s0:s0 + 32, :], rope[s0:s0 + 32, 1, :], ALU.mult))
                step.wait()
                dve.wait_ge(cos_ready, k + 1)
                nc.vector.tensor_tensor(qk_b[:, k, :], rot_cos[:, :], rot_sin[:, :], ALU.add).then_inc(rotated, 1)
            split_lo(Lin(U_MIX + 19))

            for t in range(len(TILES) + 4):
                if t < len(TILES):
                    kind, m, j, e = TILES[t]
                    nk = tile_keys(t)
                    h = 2 * m + e if kind == "a" else m + 4 * e
                    dve.wait_ge(scored, t + 1)
                    if kind == "a" and j == 0:
                        dve.wait_ge(bias_loaded[h % 2], 16 * (h // 2 + 1))
                    if kind == "a":
                        table = bias[:, h % 2, BIAS_OF[j] * 256:(BIAS_OF[j] + 1) * 256]
                    else:
                        off = 0 if j > 0 else P
                        table = mask_b[:, off:off + nk]
                    r = row[:, t % 2, :]
                    nc.vector.scalar_tensor_tensor(score[:, t % 2, 0:nk], bank[3 + t % 2][:, 0:nk], SCALE, table,
                                                   ALU.mult, ALU.add).then_inc(biased, 1)
                    dve.wait_ge(biased, t + 1)
                    step(nc.vector.reduce_max(r[:, 0:1], score[:, t % 2, 0:nk], AX_X))
                    step.wait()
                    if kind == "a":
                        nc.vector.tensor_scalar(r[:, 1:2], r[:, 0:1], -1.0, None, ALU.mult).then_inc(row_max_ready, 1)
                    else:
                        nc.vector.tensor_scalar(r[:, 1:2], r[:, 0:1], vecs[:, V_SINK + h:V_SINK + h + 1], -1.0,
                                                ALU.max, ALU.mult).then_inc(row_max_ready, 1)
                if 1 <= t < len(TILES) + 1:
                    s = t - 1
                    kind = TILES[s][0]
                    nk = tile_keys(s)
                    r = row[:, s % 2, :]
                    dve.wait_ge(exp_ready, s + 1)
                    if kind == "a":
                        step(nc.vector.reciprocal(r[:, 5:6], r[:, 2:3]))
                    else:
                        step(nc.vector.tensor_tensor(r[:, 4:5], r[:, 2:3], r[:, 3:4], ALU.add))
                        step.wait()
                        step(nc.vector.reciprocal(r[:, 5:6], r[:, 4:5]))
                    step.wait()
                    nc.vector.tensor_scalar(prob[:, s % 2, 0:nk], prob[:, s % 2, 0:nk], r[:, 5:6], None, ALU.mult)\
                      .then_inc(prob_ready, 1)
                if t >= 4 and (t - 4) % 2 == 1:
                    s = t - 4
                    kind, m, j, e = TILES[s]
                    dve.wait_ge(att_hi_ready, s // 2 + 1)
                    o = bank[(s // 2) % 2][:, 0:P]
                    if kind == "a":
                        lo_part(grid(ya_lo[:, m, :], 16 * j, 16), o.rearrange("p (r c) -> p r c", r=8),
                                grid(ya_hi[:, m, :], 16 * j, 16)).then_inc(att_lo_ready, 1)
                    else:
                        lo_part(yb_lo[:, m, j * P:(j + 1) * P], o, yb_hi[:, m, j * P:(j + 1) * P]).then_inc(att_lo_ready, 1)

            with dve.Fori(0, DC // 2) as i:
                for e in range(2):
                    n, g = Lin(U_MERGE0 + 3 * e, 6, i), Lin(G_MERGE0 + 4 * e, 8, i)
                    for k in range(2):
                        split_lo(n + k + 2)
                        unit_done(n + k)
                        nc.vector.tensor_tensor(gate_pre[:, k, :], bank[k][:, :], rstd[:, :], ALU.mult).then_inc(bank_read, 1)
                    split_lo(n + 4)
                    unit_done(n + 2)
                    dve.wait_ge(sig_ready, Lin(2 * e + 2, 4, i).v())
                    for k in range(2):
                        nc.vector.tensor_tensor(branch[:, k, :], bank[3 + k][:, :], gate_sig[:, k, :], ALU.mult)\
                          .then_inc(bank_read, 1)
                    dve.wait_ge(bank_read, (g + 6).v())
                    nc.vector.tensor_tensor(merged[:, :], branch[:, 0, :], branch[:, 1, :], ALU.add).then_inc(merged_ready, 1)
                    dve.wait_ge(merged_hi_ready, Lin(e + 1, 2, i).v())
                    m = Lin(e, 2, i)
                    lo_part(at_chunk(merged_lo, m), merged[:, :].unsqueeze(1), at_chunk(merged_hi, m)).then_inc(merged_lo_ready, 1)
            with dve.Fori(0, DC // 2) as i:
                for e in range(2):
                    n, g = Lin(U_WOUT0 + e, 2, i), Lin(G_WOUT0 + e, 2, i)
                    split_lo(n + 2)
                    unit_done(n)
                    add_to_x(Lin(e, 2, i), g, 1.0)
                    u_lo_chunk(2, Lin(e, 2, i), V_FFN2)

            ffn(1, 2, None, 0, U_FFN2, G_FFN2)
            norm_rstd(3)
            for m in range(DC):
                nc.vector.scalar_tensor_tensor(x[:, m, :], x[:, m, :], vecs[:, V_FINAL + m:V_FINAL + m + 1], rstd[:, :],
                                               ALU.mult, ALU.mult).then_inc(x_scaled, 1)
            for m in range(DC):
                u_lo_chunk(3, Lin(m), V_LN0)
            norm_rstd(4)

            n, g = Lin(U_GATES), Lin(G_GATES)
            split_lo(n + 2)
            unit_done(n)
            gb = bank[g.slot]
            i_row, f_row, f_abs, f_exp, f_log, a_row, cum_f, neg_m, m_row, e_row = g_rows
            step(nc.vector.tensor_tensor(i_row[:, :], gb[0:4, :], rstd[0:4, :], ALU.mult))
            nc.vector.tensor_tensor(f_row[:, :], gb[32:36, :], rstd[32:36, :], ALU.mult).then_inc(bank_read, 1)
            step.wait()
            step(nc.vector.tensor_scalar(i_row[:, :], i_row[:, :], vecs[0:4, V_BIF:V_BIF + 1], None, ALU.add))
            dve.wait_ge(bank_read, G_GATES + 3)
            step(nc.vector.tensor_scalar(f_row[:, :], f_row[:, :], vecs[0:4, V_BIF + 1:V_BIF + 2], None, ALU.add))
            step.wait()
            nc.vector.scalar_tensor_tensor(f_abs[:, :], f_row[:, :], -1.0, f_row[:, :], ALU.mult, ALU.max).then_inc(f_abs_ready, 1)

            def inner_scaled(n, g, c):
                split_lo(n + 2)
                unit_done(n)
                scaled(xm[:, c, 3:T + 3], g).then_inc(bank_read, 1)

            def inner_lo(of, h, c):
                dve.wait_ge(xm_hi_ready, of(4 * h + c + 1, 4).v())
                lo_part(xm_lo[:, c, :], xm[:, c, 3:T + 3], xm_hi[:, c, :]).then_inc(xm_lo_ready, 1)

            def inner_conv(of, h, g, c):
                dve.wait_ge(bank_read, (g + 3).v())
                if c > 0:
                    dve.wait_ge(xc_ready, of(4 * h + c, 4).v())
                convolve(conv[:, :], xm, lambda j: hvec[:, 4 * c + j:4 * c + j + 1], hvec[:, 16 + c:17 + c], c)\
                    .then_inc(conv_ready, 1)

            def first(c, m):
                return Lin(c)

            h0, gh0 = Lin(U_HEAD0), Lin(G_HEAD0)
            inner_scaled(h0, gh0, 0)
            dve.wait_ge(gates_act, 2)
            step(nc.vector.scalar_tensor_tensor(f_log[:, :], f_row[:, :], 0.0, f_log[:, :], ALU.min, ALU.subtract))
            step(nc.vector.memset(f_abs[:, :], 1.0))
            step.wait()
            step(nc.vector.tensor_tensor_scan(cum_f[:, :], f_abs[:, :], f_log[:, :], 0.0, ALU.mult, ALU.add))
            step.wait()
            nc.vector.tensor_tensor(a_row[:, :], i_row[:, :], cum_f[:, :], ALU.subtract).then_inc(gates_dve, 1)
            dve.wait_ge(gates_dve, 1)
            step(nc.vector.tensor_tensor_scan(m_row[:, :], f_abs[:, :], a_row[:, :], 0.0, ALU.mult, ALU.max))
            step.wait()
            nc.vector.tensor_scalar(neg_m[:, :], m_row[:, :], -1.0, None, ALU.mult).then_inc(gates_dve, 1)
            dve.wait_ge(gates_dve, 2)
            nc.vector.tensor_tensor(m_row[:, :], cum_f[:, :], m_row[:, :], ALU.add).then_inc(gates_dve, 1)
            inner_scaled(h0 + 1, gh0 + 1, 1)
            inner_lo(first, 0, 0)
            for c in range(4):
                step(nc.vector.memset(xm[:, c, 0:3], 0.0))
            step(nc.vector.tensor_copy(hvec[:, :], vecs[:, V_HEAD:V_HEAD + V_PER_HEAD]))
            step.wait()
            inner_conv(first, 0, gh0, 0)
            dve.wait_ge(gates_pe, 1)
            step(nc.vector.tensor_copy(a_col[:, :, :], bank[3][:, 0:16].rearrange("p (t h) -> p t h", t=4)))
            for k, dst in enumerate((neg_max, floor)):
                for h in range(M_HEADS):
                    dve.wait_ge(gates_pe, 4 * k + h + 2)
                    nc.vector.tensor_copy(dst[:, h, :], bank[4 + h][:, :]).then_inc(gates_dve, 1)
                inner_scaled(h0 + 2 + k, gh0 + 2 + k, 2 + k)
                inner_lo(first, 0, 1 + k)
                inner_conv(first, 0, gh0 + 1 + k, 1 + k)
            inner_lo(first, 0, 3)
            inner_conv(first, 0, gh0 + 3, 3)

            def head(i):
                of = of_head(i)
                n0, g0 = of(U_HEAD0, U_HEAD), of(G_HEAD0, G_HEAD)
                at = of(0, 1).v()
                step(nc.vector.tensor_copy(a_head[:, :].unsqueeze(2), a_col[:, :, bass.ds(at, 1)]))
                def gate_scaled(j, n, g):
                    split_lo(n + 2)
                    unit_done(n)
                    if j >= 2:
                        dve.wait_ge(oz_ready, of(j - 1, 8).v())
                    scaled(pre[:, j % 2, :], g).then_inc(bank_read, 1)

                def xc_lo_part(c):
                    dve.wait_ge(xc_hi_ready, of(c + 1, 4).v())
                    lo_part(xy_lo[:, c, :], xc[:, c, :], xy_hi[:, c, :]).then_inc(xc_lo_ready, 1)

                for c in range(4):
                    xc_lo_part(c)
                gate_scaled(0, n0 + 4, g0 + 4)
                gate_scaled(1, n0 + 5, g0 + 5)
                step.wait()
                for si in range(4):
                    nc.vector.tensor_scalar(sw[:, si, si * P:T].unsqueeze(1), neg_max[:, bass.ds(at, 1), si * P:T],
                                            a_head[:, si:si + 1], 0.0, ALU.add, ALU.min).then_inc(w_arg, 1)
                for k in range(2):
                    split_lo(n0 + 8 + k)
                    unit_done(n0 + 6 + k)
                    for e in range(2):
                        g = g0 + 6 + 2 * k + e
                        dst = (q_m, k_m)[k][:, e, :]
                        nc.vector.tensor_scalar(dst, bank[g.slot][:, :], M_DK ** -0.5 if k == 0 else 1.0, None, ALU.mult)\
                          .then_inc(bank_read, 1)
                gate_scaled(2, n0 + 8, g0 + 10)
                for si in range(4):
                    dve.wait_ge(s_ready, of(si + 1, 4).v())
                    dve.wait_ge(w_masked, of(si + 1, 4).v())
                    nc.vector.tensor_tensor(sw[:, si, si * P:T], bank[3 + si % 2][:, si * P:T], sw[:, si, si * P:T], ALU.mult)\
                      .then_inc(sw_ready, 1)
                split_lo(n0 + 11)
                split_lo(n0 + 12)
                gate_scaled(3, n0 + 11, g0 + 11)
                dve.wait_ge(den_abs, of(1, 1).v())
                step(nc.vector.tensor_tensor(den[:, :].unsqueeze(1), den[:, :].unsqueeze(1), floor[:, bass.ds(at, 1), :], ALU.max))
                step.wait()
                step(nc.vector.reciprocal(den[:, :], den[:, :]))
                step.wait()
                dve.wait_ge(oz_ready, of(4, 8).v())
                for c in range(4):
                    step(nc.vector.tensor_tensor(hh[:, c, :], o_sig[:, c, :], den[:, :], ALU.mult))
                step.wait()
                for c in range(4):
                    dve.wait_ge(num_ready, of(c + 1, 4).v())
                    nc.vector.tensor_tensor(hh[:, c, :], bank[4 + c][:, :], hh[:, c, :], ALU.mult).then_inc(h_ready, 1)
                def centred(c):
                    nc.vector.scalar_tensor_tensor(hh[:, c, :], stat[:, :], -1.0 / M_DV, hh[:, c, :], ALU.mult, ALU.add)\
                      .then_inc(h_centred, 1)

                def skip_z(c):
                    dve.wait_ge(oz_ready, of(5 + c, 8).v())
                    step(nc.vector.scalar_tensor_tensor(xc[:, c, :], xc[:, c, :], hvec[:, 24 + c:25 + c], z_act[:, c, :],
                                                        ALU.mult, ALU.mult))

                def norm_z(c):
                    dve.wait_ge(h_sq_ready, of(c + 1, 4).v())
                    step(nc.vector.scalar_tensor_tensor(hh[:, c, :], hh[:, c, :], hvec[:, 20 + c:21 + c], z_act[:, c, :],
                                                        ALU.mult, ALU.mult))

                gate_scaled(4, n0 + 12, g0 + 12)
                dve.wait_ge(h_ready, of(4, 4).v())
                dve.wait_ge(m_stat, of(1, 2).v())
                for c in range(4):
                    centred(c)
                gate_scaled(5, n0 + 13, g0 + 13)
                skip_z(0)
                skip_z(1)
                norm_z(0)
                norm_z(1)
                gate_scaled(6, n0 + 14, g0 + 14)
                skip_z(2)
                norm_z(2)
                dve.wait_ge(m_rms, of(1, 1).v())
                step(nc.vector.reciprocal(den[:, :], den[:, :]))
                gate_scaled(7, n0 + 15, g0 + 15)
                skip_z(3)
                norm_z(3)
                step.wait()
                def y(c):
                    step(nc.vector.tensor_tensor(hh[:, c, :], hh[:, c, :], den[:, :], ALU.mult))
                    step.wait()
                    nc.vector.tensor_tensor(hh[:, c, :], hh[:, c, :], xc[:, c, :], ALU.add).then_inc(y_ready, 1)

                def y_lo(c):
                    dve.wait_ge(y_hi_ready, of(c + 1, 4).v())
                    lo_part(xy_lo[:, c, :], hh[:, c, :], xy_hi[:, c, :]).then_inc(y_lo_ready, 1)

                if i is not None:
                    step(nc.vector.tensor_copy(hvec[:, :], vecs[:, bass.ds(i * V_PER_HEAD + V_HEAD + V_PER_HEAD, V_PER_HEAD)]))
                y(0)
                y(1)
                y_lo(0)
                n_out, g_out = n0 + 16, g0 + 16
                if i is not None:
                    inner_scaled(n0 + 16, g0 + 16, 0)
                    n_out, g_out = n0 + 20, g0 + 20
                y(2)
                y_lo(1)
                y(3)
                y_lo(2)
                if i is not None:
                    inner_scaled(n0 + 17, g0 + 17, 1)
                    inner_lo(of, 1, 0)
                y_lo(3)
                if i is not None:
                    for c in range(2, 4):
                        inner_scaled(n0 + 16 + c, g0 + 16 + c, c)
                        inner_lo(of, 1, c - 1)
                        inner_conv(of, 1, g0 + 14 + c, c - 2)
                    inner_lo(of, 1, 3)
                for k in range(4):
                    split_lo(n_out + 2 + k)
                    unit_done(n_out + k)
                    for e in range(2):
                        add_to_x(Lin(2 * k + e), g_out + 2 * k + e, 1.0, OUT_BANKS[(2 * k + e) % 4])
                    if i is None:
                        for m in range(2 * k, 2 * k + 2):
                            u_lo_chunk(4, Lin(m), V_LN1)
                    if i is not None and k < 2:
                        inner_conv(of, 1, g0 + 18 + k, k + 2)

            with dve.Fori(0, M_HEADS - 1) as i, step.turns(i, M_HEADS - 1, 2 + 4 * 3 + 6 + 8 + 1 + 4):
                head(i)
            head(None)

            norm_rstd(5)

            lam = vecs[:, V_PAIR:V_ALL].rearrange("p (a b) -> p a b", b=V_PER_PAIR)[:, :, 21:24]
            rates = [rate[:, k, :].rearrange("p (a b) -> p a b", b=3) for k in range(5)]
            nc.vector.scalar_tensor_tensor(rates[0], lam, -1.0, lam, ALU.mult, ALU.max).then_inc(rate_dve, 1)
            step(nc.vector.tensor_scalar(rates[3], lam, -1.0, 0.0, ALU.mult, ALU.max))
            dve.wait_ge(rate_act, 2)
            step.wait()
            step(nc.vector.tensor_tensor(rates[2], rates[3], rates[2], ALU.add))
            step.wait()
            step(nc.vector.tensor_scalar(rates[3], rates[2], -LRU_C, None, ALU.mult))
            step(nc.vector.tensor_scalar(rates[4], rates[2], LRU_C, None, ALU.mult))
            for c in range(3):
                step(nc.vector.memset(xr[:, c, 0:3], 0.0))
            def b_square(k3):
                for c in range(3):
                    dve.wait_ge(a_squared, (k3 + (c + 1)).v())
                    nc.vector.scalar_tensor_tensor(tanh[:, c, :], rgate[:, c, :], 1.0, tanh[:, c, :], ALU.add, ALU.mult)\
                        .then_inc(b_squared, 1)

            def scan(k3, c):
                dve.wait_ge(b_root, (k3 + (c + 1)).v())
                step(nc.vector.tensor_tensor(igate[:, c, :], tanh[:, c, :], igate[:, c, :], ALU.mult))
                step.wait()
                nc.vector.tensor_tensor_scan(rgate[:, c, :], decay[:, c, :], igate[:, c, :], 0.0, ALU.mult, ALU.add)\
                    .then_inc(h_scanned, 1)

            def ry_lo_part(k3, c, at):
                dve.wait_ge(ry_hi_ready, (k3 + (c + 1)).v())
                lo_part(ry_lo[:, at(c), :], tanh[:, c:c + 1, :], ry_hi[:, at(c), :]).then_inc(ry_lo_ready, 1)

            def pair(n0, g0, k3, k6, vec_at, rate_at, before):
                if before is not None:
                    dve.wait_ge(r_act, k6.v())
                step.wait()
                step(nc.vector.tensor_copy(pvec[:, :], vecs[:, vec_at]))
                step(nc.vector.tensor_copy(pair_rate[:, :, :], rate[:, 3:5, rate_at]))
                step.wait()
                for c in range(3):
                    split_lo(n0 + c + 2)
                    unit_done(n0 + c)
                    scaled(xr[:, c, 3:T + 3], g0 + c).then_inc(bank_read, 1)
                    if before is not None:
                        dve.wait_ge(ix_ready, (k3 + (c - 2)).v())
                    dve.wait_ge(bank_read, (g0 + c + 3).v())
                    convolve(rc[:, c, :], xr, lambda j: pvec[:, 4 * c + j:4 * c + j + 1], pvec[:, 12 + c:13 + c], c)\
                        .then_inc(rconv_ready, 1)
                    if c > 0:
                        rc_lo_part(c - 1, k3)
                rc_lo_part(2, k3)
                if before is not None:
                    b_square(k3 + (-3))
                for c in range(3):
                    if before is not None:
                        scan(k3 + (-3), c)
                    split_lo(n0 + c + 5)
                    unit_done(n0 + 3 + c)
                    if c == 2:
                        dve.wait_ge(g_ready, (k3 + 1).v())
                    scaled(g_pre[:, c % 2, :], g0 + 3 + c).then_inc(bank_read, 1)
                    if before is not None:
                        ry_lo_part(k3 + (-3), c, before)
                for k in range(2):
                    split_lo(n0 + 8 + k)

            def rc_lo_part(c, k3):
                dve.wait_ge(rc_hi_ready, (k3 + (c + 1)).v())
                lo_part(rc_lo[:, c, :], rc[:, c, :], rc_hi[:, c, :]).then_inc(rc_lo_ready, 1)

            pair(Lin(U_PAIR0), Lin(G_PAIR0), Lin(0), Lin(0), slice(V_PAIR, V_PAIR + V_PER_PAIR), slice(0, 3), None)
            with dve.Fori(0, 3) as i, step.turns(i, 3, 2 + 3 * 3 + 3):
                pair(Lin(U_PAIR0 + U_PAIR, U_PAIR, i), Lin(G_PAIR0 + G_PAIR, G_PAIR, i), Lin(3, 3, i), Lin(6, 6, i),
                     bass.ds(i * V_PER_PAIR + (V_PAIR + V_PER_PAIR), V_PER_PAIR), bass.ds(i * 3 + 3, 3),
                     lambda c: bass.ds(i * 3 + c, 1))
            b_square(Lin(9))
            for c in range(3):
                scan(Lin(9), c)
            for c in range(3):
                ry_lo_part(Lin(9), c, lambda c: slice(9 + c, 10 + c))
            for k in range(2 * DC):
                split_lo(Lin(U_ROUT + 2 + k))
                if k >= DC:
                    m = k - DC
                    unit_done(Lin(U_ROUT + k))
                    add_to_x(Lin(m), Lin(G_ROUT + m), 1.0, m)
            norm_rstd(6)
            for m in range(DC):
                nc.vector.scalar_tensor_tensor(x[:, m, :], x[:, m, :], vecs[:, V_FINAL2 + m:V_FINAL2 + m + 1], rstd[:, :],
                                               ALU.mult, ALU.mult).then_inc(out_ready, 1)

        @block.gpsimd
        def _(pool):
            step = Steps(pool, pool_step)

            def norm_sum(q):
                if q > 0:
                    pool.wait_ge(stat_ready, q)
                nc.gpsimd.memset(sumsq[:, :], 0.0).then_inc(sq_added, 1)
                for m in range(DC):
                    pool.wait_ge(sq_ready, DC * q + m + 1)
                    pool.wait_ge(sq_added, 9 * q + m + 1)
                    nc.gpsimd.tensor_tensor(sumsq[:, :], sumsq[:, :], sq[:, m % 2, :], ALU.add).then_inc(sq_added, 1)

            norm_sum(0)
            norm_sum(1)
            pool.wait_ge(stat_ready, 2)
            pool.dma_start(rope[:, :, :], rope_in).then_inc(tab_loaded, 16)
            pool.dma_start(mask_b[:, :], maskb_in).then_inc(tab_loaded, 16)
            for h in range(2):
                pool.dma_start(bias[:, h, :], bias_in[h]).then_inc(bias_loaded[h], 16)
            pool.wait_ge(tab_loaded, 32)
            for k in range(5):
                pool.wait_ge(bank_read, G_MIX + 8 + k + 3)
                if k > 0:
                    pool.wait_ge(rotated, k)
                nc.gpsimd.tensor_tensor(rot_cos[:, :], unrot[:, :], rope[:, 0, :], ALU.mult).then_inc(cos_ready, 1)
                if k == 0:
                    pool.wait_ge(va_ready, 4)
                if k < 4:
                    for r in range(4):
                        p0 = (r % 2) * 64 + KEY_COL0[k]
                        pool.dma_start(v_win[32 * r:32 * r + 32, k, :, :], v_a[p0:p0 + 32, r // 2::2, :]).then_inc(v_moved, 16)
            for h in range(2, 8):
                pool.wait_ge(biased, 8 * (h // 2))
                pool.dma_start(bias[:, h % 2, :], bias_in[h]).then_inc(bias_loaded[h % 2], 16)
            for q in range(2, 4):
                norm_sum(q)
            pool.wait_ge(stat_ready, 4)
            pool.dma_start(sel[:, :, :], sel_in).then_inc(sel_loaded, 16)
            pool.dma_start(causal[:, :], causal_in).then_inc(causal_loaded, 16)
            norm_sum(4)

            pool.wait_ge(causal_loaded, 16)
            with pool.Fori(0, M_HEADS) as i, step.turns(i, M_HEADS, 2):
                for si in range(4):
                    pool.wait_ge(w_exp, Lin(si + 1, 4, i).v())
                    dia = sw[:, si, si * P:(si + 1) * P]
                    nc.gpsimd.tensor_tensor(dia, dia, causal[:, :], ALU.mult).then_inc(w_masked, 1)
                pool.wait_ge(h_ready, Lin(2, 4, i).v())
                step(nc.gpsimd.tensor_tensor(hsum[:, :], hh[:, 0, :], hh[:, 1, :], ALU.add))
                pool.wait_ge(h_ready, Lin(3, 4, i).v())
                step.wait()
                step(nc.gpsimd.tensor_tensor(hsum[:, :], hsum[:, :], hh[:, 2, :], ALU.add))
                pool.wait_ge(h_ready, Lin(4, 4, i).v())
                step.wait()
                nc.gpsimd.tensor_tensor(hsum[:, :], hsum[:, :], hh[:, 3, :], ALU.add).then_inc(h_summed, 1)
                for c in range(1, 4):
                    pool.wait_ge(h_sq_ready, Lin(c + 1, 4, i).v())
                    if c > 1:
                        pool.wait_ge(h_squared, Lin(c - 1, 3, i).v())
                    nc.gpsimd.tensor_tensor(hsum[:, :], sq[:, 0, :] if c == 1 else hsum[:, :], sq[:, c % 2, :], ALU.add)\
                        .then_inc(h_squared, 1)
            pool.wait_ge(m_stat, 2 * M_HEADS)
            norm_sum(5)
            with pool.Fori(0, 4) as i:
                for c in range(3):
                    pool.wait_ge(rgates, Lin(c + 4, 6, i).v())
                    nc.gpsimd.tensor_tensor(igate[:, c, :], igate[:, c, :], rc[:, c, :], ALU.mult).then_inc(ix_ready, 1)
                for c in range(3):
                    pool.wait_ge(r_act, Lin(2 * c + 2, 6, i).v())
                    nc.gpsimd.tensor_tensor(rgate[:, c, :], decay[:, c, :], decay[:, c, :], ALU.mult).then_inc(a_squared, 1)
                for c in range(3):
                    pool.wait_ge(h_scanned, Lin(c + 1, 3, i).v())
                    nc.gpsimd.tensor_tensor(tanh[:, c, :], rgate[:, c, :], g_act[:, c, :], ALU.mult).then_inc(ry_ready, 1)
            norm_sum(6)


def blocks(w, pairs):
    import numpy as np
    u = np.zeros((P, UB * P), np.float32)
    for k, (r, c) in enumerate(pairs):
        u[:, k * P:(k + 1) * P] = w[r * P:(r + 1) * P, c * P:(c + 1) * P]
    return u


def wide(w, r0):
    import numpy as np
    return np.concatenate([w[r0 * P:(r0 + 1) * P], w[(r0 + 1) * P:(r0 + 2) * P]], axis=1)


def weight_stream(a):
    import numpy as np
    units = []

    def columns(w, c, rows=range(8)):
        units.append(blocks(w, [(r, c) for r in rows]))

    def ffn(gate_w, up_w, down_w):
        for c in range(F_CHUNKS):
            columns(gate_w, c)
            columns(up_w, c)
        for c in range(DC):
            for part in range(3):
                columns(down_w, c, range(8 * part, min(8 * part + 8, F_CHUNKS)))

    order = np.concatenate([np.arange(HD * h, HD * (h + 1)) for j in range(4) for h in (j, j + 4)])
    ffn(a["ffn1_w_gate"][0], a["ffn1_w_up"][0], a["ffn1_w_down"][0])
    w = a["w_in"][0]
    for c in range(8):
        columns(w, c)
    for part in range(4):
        units.append(wide(w[:, 1024:1536], 2 * part))
    qb = w[:, 1536:2048][:, order]
    for c in range(4):
        columns(qb, c)
    columns(w, 16)
    columns(w, 17)
    wb = a["w_branch_b"][0][order]
    for c in range(DC):
        columns(w, 18 + c)
        columns(w, 26 + c)
        units.append(np.concatenate([blocks(a["w_branch_a"][0], [(r, c) for r in range(4)])[:, :4 * P],
                                     blocks(wb, [(r, c) for r in range(4)])[:, :4 * P]], axis=1))
    for c in range(DC):
        columns(a["w_out"][0], c)
    ffn(a["ffn2_w_gate"][0], a["ffn2_w_up"][0], a["ffn2_w_down"][0])

    w = a["m_w_in_2"][0]
    gates = np.zeros((D, P), np.float32)
    gates[:, 0:4] = w[:, 6144:6148]
    gates[:, 32:36] = w[:, 6148:6152]
    columns(gates, 0)
    for c in range(4):
        columns(w, c)
    for h in range(M_HEADS):
        z_gate, o_gate = 16 + 4 * h, 32 + 4 * h
        columns(w, o_gate)
        columns(w, o_gate + 1)
        for wk in (a["m_w_q_2"][0, h], a["m_w_k_2"][0, h]):
            units.append(blocks(wk, [(r, e) for e in range(2) for r in range(4)]))
        columns(w, o_gate + 2)
        for part in range(2):
            units.append(wide(a["m_w_v_2"][0, h], 2 * part))
        columns(w, o_gate + 3)
        for c in range(4):
            columns(w, z_gate + c)
        if h < M_HEADS - 1:
            for c in range(4):
                columns(w, 4 * (h + 1) + c)
        for k in range(4):
            units.append(blocks(a["m_w_out_2"][0], [(4 * h + r, 2 * k + e) for e in range(2) for r in range(4)]))
    w = a["r_w_in_2"][0]
    for p in range(4):
        for base in (0, 12):
            for c in range(3):
                columns(w, base + 3 * p + c)
        for wg in (a["r_w_a_2"][0], a["r_w_x_2"][0]):
            pair = np.zeros((3 * P, 3 * P), np.float32)
            pair[0:192, 0:192] = wg[2 * p]
            pair[192:384, 192:384] = wg[2 * p + 1]
            units.append(blocks(pair, GATE_BLOCKS))
    for part in range(2):
        for c in range(DC):
            columns(a["r_w_out_2"][0], c, range(6 * part, 6 * part + 6))
    while len(units) < U_ALL:
        units.append(np.zeros((P, UB * P), np.float32))
    assert len(units) == U_ALL
    return np.stack(units)


def vectors(a):
    import numpy as np
    v = np.zeros((P, V_ALL), np.float32)

    def put(col, vec):
        v[:, col:col + len(vec) // P] = vec.reshape(-1, P).T

    for col, vec in ((V_FFN1, a["ffn1_norm"][0]), (V_MIX, a["mix_norm"][0]), (V_FFN2, a["ffn2_norm"][0]),
                     (V_FINAL, a["final_norm"]), (V_LN0, a["ln_g_2"][0]), (V_LN1, a["ln_g_2"][1]),
                     (V_FINAL2, a["final_g_2"])):
        put(col, vec)
    v[:, V_SINK:V_SINK + 8] = a["sink_logit"][0][None, :]
    v[0:4, V_BIF] = a["m_b_i_2"][0]
    v[0:4, V_BIF + 1] = a["m_b_f_2"][0]
    for h in range(M_HEADS):
        col, part = V_HEAD + h * V_PER_HEAD, slice(h * M_DV, (h + 1) * M_DV)
        for c in range(4):
            for j in range(4):
                put(col + 4 * c + j, a["m_conv_w_2"][0, j, part][c * P:(c + 1) * P])
        put(col + 16, a["m_conv_b_2"][0, part])
        put(col + 20, a["m_norm_w_2"][0, part])
        put(col + 24, a["m_skip_2"][0, part])
    for p in range(4):
        col, part = V_PAIR + p * V_PER_PAIR, slice(p * 3 * P, (p + 1) * 3 * P)
        for c in range(3):
            for j in range(4):
                put(col + 4 * c + j, a["r_conv_w_2"][0, j, part][c * P:(c + 1) * P])
        for k, name in enumerate(("r_conv_b_2", "r_b_a_2", "r_b_x_2", "r_lam_2")):
            put(col + 12 + 3 * k, a[name][0, part])
    return v


def neighbourhood_bias(rpb):
    import numpy as np
    out = np.full((8, P, 3, 256), -1e30, np.float32)
    for kind, j in enumerate((0, 1, 3)):
        for c in range(16):
            col = 16 * j + c
            start = min(max(col - 8, 0), 64 - 16)
            k0 = start - KEY_COL0[j]
            for r in range(8):
                for i in range(8):
                    out[:, r * 16 + c, kind, i * 32 + k0:i * 32 + k0 + 16] = \
                        rpb[:, i - r + 7, start - col + 15:start - col + 31]
    return out.reshape(8, P, 768)


def tables():
    import numpy as np
    half = HD // 2
    inv = np.float32(10000.0) ** (-np.arange(half, dtype=np.float32) / np.float32(half))
    ang = (np.arange(T, dtype=np.float32)[None, :] * inv[:, None].astype(np.float32)).astype(np.float32)
    cos, sin = np.cos(ang).astype(np.float32), np.sin(ang).astype(np.float32)
    rope = np.stack([np.tile(cos, (4, 1)), np.concatenate([sin, -sin, sin, -sin])], axis=1)
    q, k = np.arange(P)[:, None], np.arange(P)[None, :]
    far = np.float32(-1e30)
    mask = np.concatenate([np.where(k >= q, 0, far), np.zeros((P, P)), np.where(k <= q, 0, far)], axis=1).astype(np.float32)
    sel = np.zeros((4, M_HEADS, P), np.float32)
    for h in range(M_HEADS):
        sel[h, h, :] = 1
    return rope.astype(np.float32), mask, np.eye(P, dtype=np.float32), sel, np.where(k >= q, 1, 0).astype(np.float32)


def kernel(**inputs):
    import numpy as np
    import concourse.bacc as bacc
    from concourse.bass_utils import run_bass_kernel_spmd

    a = {k: np.asarray(v) for k, v in inputs.items()}
    rope, mask, ident, sel, causal = tables()
    arrays = {
        "x_t": np.ascontiguousarray(a["x"][0].T),
        "weights": weight_stream(a),
        "vectors": vectors(a),
        "neighbour_bias": neighbourhood_bias(a["na_rpb"][0]),
        "rope_table": rope, "band_mask": mask, "identity": ident, "head_rows": sel, "causal_mask": causal,
    }
    nc = bacc.Bacc("TRN2", target_bir_lowering=False, num_devices=1)
    args = [nc.dram_tensor(n, v.shape, F32, kind="ExternalInput").ap() for n, v in arrays.items()]
    out = nc.dram_tensor("out_t", (D, T), F32, kind="ExternalOutput").ap()
    build_program(nc, *args, out)
    got = run_bass_kernel_spmd(nc, [arrays], core_ids=[0]).results[0]["out_t"]
    return np.ascontiguousarray(got.T)[None]
```
